# Optimizing a Trainium2 kernel written in Bass

```python
import math
import jax
import jax.numpy as jnp
from jax import lax
import numpy as np

D_MODEL = 2048
BATCH = 1
SEQ = 256
DEPTH = 1
DEC_BATCH = 8
DEC_SEQ = 8
PAST_LEN = 2048
PAGE_SIZE = 128

HG_HEADS = 8
HG_DK = 128
HG_DV = 128
HG_WIDTH = HG_HEADS * HG_DV
HG_CHUNK = 64
DA_HEADS = 8
DA_DH = 64
DA_DV = 2 * DA_DH
DA_WIDTH = DA_HEADS * DA_DV
N_BUCKETS = 32
REL_MAX_DISTANCE = 128
Q_BLOCK = 128
D_FF = ((8 * D_MODEL // 3 + 255) // 256) * 256
RMS_EPS = 1e-6
NEG_INF = -1e30

_IN_SIZES = (HG_HEADS * HG_DK, HG_HEADS * HG_DK, HG_WIDTH, HG_WIDTH,
             2 * DA_HEADS * DA_DH, 2 * DA_HEADS * DA_DH, DA_WIDTH, D_MODEL, D_MODEL)
IN_SPLIT_POINTS = tuple(int(s) for s in np.cumsum(_IN_SIZES)[:-1])
N_IN = int(sum(_IN_SIZES))

kernel_name = 'hgrn2_diffattn_gated_hybrid_step'

def rms_norm(x, w):
    xf = x.astype(jnp.float32)
    y = xf * lax.rsqrt(jnp.mean(xf * xf, axis=-1, keepdims=True) + RMS_EPS)
    return (y * w.astype(jnp.float32)).astype(x.dtype)

def t5_bucket(dist):
    n = jnp.maximum(dist, 0)
    max_exact = N_BUCKETS // 2
    nf = jnp.maximum(n, 1).astype(jnp.float32)
    large = max_exact + (jnp.log(nf / max_exact) / math.log(REL_MAX_DISTANCE / max_exact)
                         * (N_BUCKETS - max_exact)).astype(jnp.int32)
    large = jnp.minimum(large, N_BUCKETS - 1)
    return jnp.where(n < max_exact, n, large)

def diff_attend(q, k, v, q_pos, k_pos, bias_table, lam):
    b, lq = q.shape[:2]
    lk = k.shape[1]
    s = jnp.einsum('bqhd,bkhd->bhqk', q.astype(jnp.float32), k.astype(jnp.float32)) * (DA_DH ** -0.5)
    bucket = t5_bucket(q_pos[:, None] - k_pos[None, :])
    s = s + jnp.transpose(bias_table.astype(jnp.float32)[bucket], (2, 0, 1))[None]
    s = jnp.where((k_pos[None, :] <= q_pos[:, None])[None, None], s, NEG_INF)
    p = jax.nn.softmax(s, axis=-1).reshape(b, 2, DA_HEADS, lq, lk)
    pd = p[:, 0] - lam * p[:, 1]
    return jnp.einsum('bhqk,bkhv->bqhv', pd, v.astype(jnp.float32))

def attend_prompt(q, k, v, bias_table, lam):
    b, L = q.shape[:2]
    nb = L // Q_BLOCK
    pos = jnp.arange(L, dtype=jnp.int32)
    kf = k.astype(jnp.float32)
    vf = v.astype(jnp.float32)
    qb = jnp.moveaxis(q.reshape(b, nb, Q_BLOCK, 2 * DA_HEADS, DA_DH), 1, 0)
    pb = pos.reshape(nb, Q_BLOCK)
    o = lax.map(lambda a: diff_attend(a[0], kf, vf, a[1], pos, bias_table, lam), (qb, pb))
    return jnp.moveaxis(o, 0, 1).reshape(b, L, DA_HEADS, DA_DV)

def hgrn2_recurrence(q, f_logit, i, lb, s0):
    b, L, H, dk = q.shape
    dv = i.shape[-1]
    f = lb + (1.0 - lb) * jax.nn.sigmoid(f_logit.astype(jnp.float32))
    g = jnp.log(f)
    kin = 1.0 - f
    c = min(HG_CHUNK, L)
    pad = (-L) % c
    n = (L + pad) // c

    def blk(t):
        t = jnp.pad(t, ((0, 0), (0, pad), (0, 0), (0, 0)))
        return t.reshape(b, n, c, H, t.shape[-1]).transpose(0, 3, 1, 2, 4)

    qc = blk(q.astype(jnp.float32))
    kc = blk(kin)
    vc = blk(i.astype(jnp.float32))
    G = jnp.cumsum(blk(g), axis=3)
    qg = qc * jnp.exp(G)
    kg = kc * jnp.exp(-G)
    causal = jnp.tril(jnp.ones((c, c), dtype=bool))
    A = jnp.where(causal, jnp.einsum('bhncd,bhnsd->bhncs', qg, kg), 0.0)
    o_intra = jnp.einsum('bhncs,bhnsv->bhncv', A, vc)
    G_last = G[:, :, :, -1]
    dS = jnp.einsum('bhncd,bhncv->bhndv', kc * jnp.exp(G_last[:, :, :, None, :] - G), vc)
    decay = jnp.exp(G_last)

    def step(S, xs):
        d, ds = xs
        return d[..., None] * S + ds, S

    s_final, s_prev = lax.scan(step, s0.astype(jnp.float32),
                               (jnp.moveaxis(decay, 2, 0), jnp.moveaxis(dS, 2, 0)))
    o_inter = jnp.einsum('bhncd,nbhdv->bhncv', qg, s_prev)
    o = (o_intra + o_inter).transpose(0, 2, 3, 1, 4).reshape(b, n * c, H, dv)[:, :L]
    return o, s_final.astype(s0.dtype)

def decoder_layer(x, l, s0, past_k, past_v, params):
    (norm_mix_pre, norm_mix_post, norm_ffn_pre, norm_ffn_post, w_in, hg_lb_logits, hg_norm_w,
     lq1, lk1, lq2, lk2, da_subln_w, rel_bias_table, w_branch_hg, w_branch_da, w_out,
     w_ffn_up, w_ffn_down) = params
    b, L, _ = x.shape
    h = rms_norm(x, norm_mix_pre[l])
    u = h @ w_in[l]
    hq, hf, hi, hgate, dq, dk, dv, g_hg, g_da = jnp.split(u, IN_SPLIT_POINTS, axis=-1)

    lb = jnp.cumsum(jax.nn.softmax(hg_lb_logits.astype(jnp.float32), axis=0), axis=0)[l]
    lb = lb.reshape(HG_HEADS, HG_DK)
    o_hg, s_new = hgrn2_recurrence(hq.reshape(b, L, HG_HEADS, HG_DK), hf.reshape(b, L, HG_HEADS, HG_DK),
                                   hi.reshape(b, L, HG_HEADS, HG_DV), lb, s0)
    o_hg = rms_norm(o_hg.astype(x.dtype), hg_norm_w[l]) * jax.nn.silu(hgate.reshape(b, L, HG_HEADS, HG_DV))
    y_hg = o_hg.reshape(b, L, HG_WIDTH) @ w_branch_hg[l]

    q = dq.reshape(b, L, 2 * DA_HEADS, DA_DH)
    k = dk.reshape(b, L, 2 * DA_HEADS, DA_DH)
    v = dv.reshape(b, L, DA_HEADS, DA_DV)
    lam_init = 0.8 - 0.6 * math.exp(-0.3 * l)
    lam = (jnp.exp(jnp.sum(lq1[l].astype(jnp.float32) * lk1[l].astype(jnp.float32)))
           - jnp.exp(jnp.sum(lq2[l].astype(jnp.float32) * lk2[l].astype(jnp.float32))) + lam_init)
    if past_k is None:
        o_da = attend_prompt(q, k, v, rel_bias_table, lam)
    else:
        past_len = past_k.shape[1]
        k_all = jnp.concatenate([past_k, k.astype(past_k.dtype)], axis=1)
        v_all = jnp.concatenate([past_v, v.astype(past_v.dtype)], axis=1)
        q_pos = past_len + jnp.arange(L, dtype=jnp.int32)
        k_pos = jnp.arange(past_len + L, dtype=jnp.int32)
        o_da = diff_attend(q, k_all, v_all, q_pos, k_pos, rel_bias_table, lam)
    o_da = rms_norm(o_da.astype(x.dtype), da_subln_w[l]) * (1.0 - lam_init)
    y_da = o_da.reshape(b, L, DA_WIDTH) @ w_branch_da[l]

    mixed = (jax.nn.sigmoid(g_hg) * y_hg + jax.nn.sigmoid(g_da) * y_da) @ w_out[l]
    x = x + rms_norm(mixed, norm_mix_post[l])

    h = rms_norm(x, norm_ffn_pre[l])
    gate, up = jnp.split(h @ w_ffn_up[l], 2, axis=-1)
    ffn = (jax.nn.silu(gate) * up) @ w_ffn_down[l]
    x = x + rms_norm(ffn, norm_ffn_post[l])
    return x, k, v, s_new

def setup_inputs(seed: int = 0) -> dict:
    key = jax.random.key(seed)
    ks = jax.random.split(key, 26)
    n_pages = PAST_LEN // PAGE_SIZE
    n_used = DEC_BATCH * n_pages
    n_pool = n_used + max(1, n_used // 4)
    f32 = jnp.float32

    def nrm(k, shape, scale):
        return jax.random.normal(k, shape, f32) * scale

    def gain(k, shape):
        return 1.0 + 0.02 * jax.random.normal(k, shape, f32)

    page_table = jax.random.permutation(ks[5], n_pool)[:n_used].reshape(DEC_BATCH, n_pages).astype(jnp.int32)
    return {
        'x_prompt': nrm(ks[0], (BATCH, SEQ, D_MODEL), 1.0),
        'x_sample': nrm(ks[1], (DEC_BATCH, DEC_SEQ, D_MODEL), 1.0),
        'cache_k': nrm(ks[2], (DEPTH, n_pool, PAGE_SIZE, 2 * DA_HEADS, DA_DH), 1.0),
        'cache_v': nrm(ks[3], (DEPTH, n_pool, PAGE_SIZE, DA_HEADS, DA_DV), 1.0),
        'state_hgrn': nrm(ks[4], (DEPTH, DEC_BATCH, HG_HEADS, HG_DK, HG_DV), 0.5),
        'page_table': page_table,
        'norm_mix_pre': gain(ks[6], (DEPTH, D_MODEL)),
        'norm_mix_post': gain(ks[7], (DEPTH, D_MODEL)),
        'norm_ffn_pre': gain(ks[8], (DEPTH, D_MODEL)),
        'norm_ffn_post': gain(ks[9], (DEPTH, D_MODEL)),
        'w_in': nrm(ks[10], (DEPTH, D_MODEL, N_IN), D_MODEL ** -0.5),
        'hg_lb_logits': nrm(ks[11], (DEPTH + 1, HG_HEADS * HG_DK), 0.1),
        'hg_norm_w': gain(ks[12], (DEPTH, HG_DV)),
        'da_lambda_q1': nrm(ks[13], (DEPTH, DA_DH), 0.1),
        'da_lambda_k1': nrm(ks[14], (DEPTH, DA_DH), 0.1),
        'da_lambda_q2': nrm(ks[15], (DEPTH, DA_DH), 0.1),
        'da_lambda_k2': nrm(ks[16], (DEPTH, DA_DH), 0.1),
        'da_subln_w': gain(ks[17], (DEPTH, DA_DV)),
        'rel_bias_table': nrm(ks[18], (N_BUCKETS, 2 * DA_HEADS), 0.5),
        'w_branch_hg': nrm(ks[19], (DEPTH, HG_WIDTH, D_MODEL), HG_WIDTH ** -0.5),
        'w_branch_da': nrm(ks[20], (DEPTH, DA_WIDTH, D_MODEL), DA_WIDTH ** -0.5),
        'w_out': nrm(ks[21], (DEPTH, D_MODEL, D_MODEL), D_MODEL ** -0.5),
        'w_ffn_up': nrm(ks[22], (DEPTH, D_MODEL, 2 * D_FF), D_MODEL ** -0.5),
        'w_ffn_down': nrm(ks[23], (DEPTH, D_FF, D_MODEL), D_FF ** -0.5),
    }

def reference(x_prompt, x_sample, cache_k, cache_v, state_hgrn, page_table, norm_mix_pre, norm_mix_post,
              norm_ffn_pre, norm_ffn_post, w_in, hg_lb_logits, hg_norm_w, da_lambda_q1, da_lambda_k1,
              da_lambda_q2, da_lambda_k2, da_subln_w, rel_bias_table, w_branch_hg, w_branch_da, w_out,
              w_ffn_up, w_ffn_down):
    params = (norm_mix_pre, norm_mix_post, norm_ffn_pre, norm_ffn_post, w_in, hg_lb_logits, hg_norm_w,
              da_lambda_q1, da_lambda_k1, da_lambda_q2, da_lambda_k2, da_subln_w, rel_bias_table,
              w_branch_hg, w_branch_da, w_out, w_ffn_up, w_ffn_down)
    n_seq, n_pages = page_table.shape
    past_len = n_pages * cache_k.shape[2]
    y_p = x_prompt
    y_s = x_sample
    kp_l, vp_l, sp_l, ks_l, vs_l, ss_l = [], [], [], [], [], []
    for l in range(DEPTH):
        s0 = jnp.zeros((x_prompt.shape[0], HG_HEADS, HG_DK, HG_DV), state_hgrn.dtype)
        y_p, kp, vp, sp = decoder_layer(y_p, l, s0, None, None, params)
        past_k = cache_k[l][page_table].reshape(n_seq, past_len, 2 * DA_HEADS, DA_DH)
        past_v = cache_v[l][page_table].reshape(n_seq, past_len, DA_HEADS, DA_DV)
        y_s, ks_, vs_, ss_ = decoder_layer(y_s, l, state_hgrn[l], past_k, past_v, params)
        kp_l.append(kp)
        vp_l.append(vp)
        sp_l.append(sp)
        ks_l.append(ks_)
        vs_l.append(vs_)
        ss_l.append(ss_)
    return (y_p, y_s, jnp.stack(kp_l), jnp.stack(vp_l), jnp.stack(sp_l),
            jnp.stack(ks_l), jnp.stack(vs_l), jnp.stack(ss_l))


_drawn_inputs = setup_inputs


def setup_inputs(seed=0):
    import zlib

    import numpy as np

    out = dict(_drawn_inputs(seed))
    spreads = {}
    factors = {'norm_mix_post': 3.429,
     'norm_ffn_pre': 3.44,
     'norm_ffn_post': 4.814,
     'hg_norm_w': 6.201,
     'da_subln_w': 4.38}
    for name, (base, spread) in spreads.items():
        noise = np.random.default_rng([zlib.crc32(name.encode()), seed]).standard_normal(out[name].shape)
        drawn = base * np.exp(spread * noise) if base else spread * noise
        out[name] = jnp.asarray(drawn.astype(out[name].dtype))
    for name, factor in factors.items():
        out[name] = (out[name] * factor).astype(out[name].dtype)
    return out
```

```python
from contextlib import ExitStack

import concourse.bass as bass
from concourse import mybir

ALU = mybir.AluOpType
ACT = mybir.ActivationFunctionType
AX_X = mybir.AxisListType.X
F32 = mybir.dt.float32
F32R = mybir.dt.float32r
I32 = mybir.dt.int32

P = 128
D_MODEL, D_FF = 2048, 5632
SEQ, NB, NQ = 256, 8, 8
T = SEQ + NB * NQ
HEADS, MAPS, DH, DV = 8, 16, 64, 128
PAGE, PAGES, POOL = 128, 16, 160
PAST = PAGE * PAGES
CHUNK, CHUNKS = 64, T // 64
N_IN = 88
QT, FT, IT, OT, DQT, DKT, DVT, GHT, GDT = 0, 8, 16, 24, 32, 40, 48, 56, 72
EPS = 1e-6
LAM_INIT = 0.2
SCALE = DH ** -0.5
KT = D_MODEL // P
FT_N = D_FF // P
RAW, HALVES = 8, 4
BIAS_L = 384
NEAR = P + NQ

SETS_IN, SETS_HEAD = 22, 14
R_IN = 0
R_HEAD = R_IN + 8 * SETS_HEAD
R_MIX = R_IN + 8 * SETS_IN
R_BRANCH = R_MIX + 2 * PAGES * NB
R_OUT = R_BRANCH + 32
R_UP = R_OUT + 32
R_DOWN = R_UP + 16 * (D_FF // 512)


class Steps:

    def __init__(self, sem, names, lead=0):
        self.sem, self.names, self.lead, self.next = sem, names.split(), lead, 0

    def at(self, rnd, name):
        return len(self.names) * (rnd + self.lead) + self.names.index(name) + 1

    def begin(self):
        self.next = 0

    def done(self, ins, name):
        assert self.names[self.next] == name, (self.names[self.next], name)
        self.next += 1
        ins.then_inc(self.sem, 1)

    def last(self, rnd):
        return self.at(rnd, self.names[-1])


def build(nc, xp, xs, ck, cv, st, pt, w_in, w_hg, w_da, w_out, w_up, w_dn, nrm, hgw, lbl, lamv,
          table, c_ident, c_scan, c_causal, c_own, c_hot, c_coef,
          y_p, y_s, k_p, v_p, h_p, k_s, v_s, h_s):
    with ExitStack() as ctx:
        def sb(name, shape, dt=F32, where=None):
            return (where or ctx).enter_context(nc.sbuf_tensor(name, shape, dt))

        def sem(name):
            return ctx.enter_context(nc.semaphore(name))

        uT = nc.dram_tensor("uT", (N_IN, P, T), F32, kind="Internal").ap()
        bias_rows = nc.dram_tensor("bias_rows", (MAPS, P, BIAS_L), F32, kind="Internal").ap()
        new_scores = nc.dram_tensor("new_scores", (MAPS, NB * NQ, NB * NQ), F32, kind="Internal").ap()
        xT_keep = nc.dram_tensor("xT_keep", (KT, P, T), F32, kind="Internal").ap()

        raw = [sb(f"raw{j}", [P, 1024]) for j in range(RAW)]
        w_hi = [sb(f"w_hi{j}", [P, 1024], F32R) for j in range(HALVES)]
        w_lo = [sb(f"w_lo{j}", [P, 1024], F32R) for j in range(HALVES)]
        ident = sb("ident", [P, P])
        ones = sb("ones", [P, P])
        nrm_w = sb("nrm_w", [P, 4, KT])
        hg_w = sb("hg_w", [P, 2])
        eps_c = sb("eps_c", [P, 1])
        coef = sb("coef", [P, 2])
        cf = sb("cf", [P, 1])
        neg_lam = sb("neg_lam", [P, 1])
        lam_s = sb("lam_s", [P, 8])
        o_all = sb("o_all", [P, KT, T])
        o_hg, o_da = o_all[:, 0:HEADS, :], o_all[:, HEADS:, :]
        stage = [sb(f"stage{j}", [P, 4, T]) for j in range(2)]
        ps = ctx.enter_context(nc.psum_tensor("ps", [P, 8, 512], F32))

        at_in = ExitStack()
        x_hi = sb("x_hi", [P, KT, T], F32R, at_in)
        x_lo = sb("x_lo", [P, KT, T], F32R, at_in)
        scan_keep = sb("scan_keep", [P, T], F32, at_in)
        causal = sb("causal", [CHUNK, CHUNKS, CHUNK], I32, at_in)
        own = sb("own", [CHUNK, NB], F32, at_in)
        lb_t = sb("lb_t", [P, 8, HEADS], F32, at_in)
        lb, omlb = lb_t[:, 6, :], lb_t[:, 7, :]
        aT = sb("aT", [CHUNK, CHUNKS, CHUNK], F32, at_in)
        at_x = ExitStack()
        x_tok = [sb(f"x_tok{j}", [P, D_MODEL], F32, at_x) for j in range(3)]
        x_sq = sb("x_sq", [P, D_MODEL], F32, at_x)
        xT4 = [sb(f"xT4_{j}", [P, 4, T], F32, at_x) for j in range(2)]
        hT = [sb(f"hT{j}", [P, T], F32, at_x) for j in range(2)]
        x_rs = sb("x_rs", [P, 3, 3], F32, at_x)
        x_rsb = sb("x_rsb", [P, 3, P], F32, at_x)
        rs_all = sb("rs_all", [P, T], F32, at_x)
        lam_in = sb("lam_in", [P, 4, DH], F32, at_x)
        lam_p = sb("lam_p", [P, 2, DH], F32, at_x)
        hot = sb("hot", [33, BIAS_L], F32, at_x)
        tab = sb("tab", [33, MAPS], F32, at_x)
        bias_vec = sb("bias_vec", [MAPS, BIAS_L], F32, at_x)
        at_x.close()
        at_h = ExitStack()
        hin = [sb(f"hin{j}", [P, 3, T], F32, at_h) for j in range(2)]
        mq = [sb(f"mq{j}", [P, T], F32, at_h) for j in range(2)]
        mk = [sb(f"mk{j}", [P, T], F32, at_h) for j in range(2)]
        mv = [sb(f"mv{j}", [P, T], F32, at_h) for j in range(2)]
        s0 = [sb(f"s0{j}", [P, NB, DV], F32, at_h) for j in range(2)]
        mb = [sb(f"mb{j}", [P, 2, 2 * P], F32, at_h) for j in range(2)]
        kin = sb("kin", [P, T], F32, at_h)
        fg = sb("fg", [P, T], F32, at_h)
        lg = sb("lg", [P, T], F32, at_h)
        G = sb("G", [P, T], F32, at_h)
        eG = sb("eG", [P, T], F32, at_h)
        kg = sb("kg", [P, T], F32, at_h)
        kd = sb("kd", [P, T], F32, at_h)
        qg = sb("qg", [P, T], F32, at_h)
        k_tok = sb("k_tok", [P, 3, P], F32, at_h)
        v_tok = sb("v_tok", [P, 3, P], F32, at_h)
        i_tok = sb("i_tok", [CHUNK, CHUNKS, DV], F32, at_h)
        kd_tok = sb("kd_tok", [CHUNK, CHUNKS, P], F32, at_h)
        i_own = sb("i_own", [CHUNK, NB, DV], F32, at_h)
        state = sb("state", [P, 4, DV], F32, at_h)
        s_new = sb("s_new", [P, NB, DV], F32, at_h)
        s_at = sb("s_at", [P, 2, 3 * P], F32, at_h)
        s_sm = sb("s_sm", [CHUNK, 2, CHUNK], F32, at_h)
        mx = sb("mx", [P, 4], F32, at_h)
        nmx = sb("nmx", [P, 4], F32, at_h)
        sm = sb("sm", [P, 4], F32, at_h)
        rc = sb("rc", [P, 4], F32, at_h)
        pd2 = sb("pd2", [P, 3 * P], F32, at_h)
        pd = sb("pd", [P, 3 * P], F32, at_h)
        pdt = sb("pdt", [P, 3, P], F32, at_h)
        at_h.close()
        at_in.close()

        at_mix = ExitStack()
        kt_hi = [sb(f"kt_hi{j}", [P, 8, 4 * PAGE], F32R, at_mix) for j in range(2)]
        kt_lo = [sb(f"kt_lo{j}", [P, 8, 4 * PAGE], F32R, at_mix) for j in range(2)]
        q_hi = sb("q_hi", [P, 8, P], F32R, at_mix)
        q_lo = sb("q_lo", [P, 8, P], F32R, at_mix)
        p_hi = sb("p_hi", [P, PAGES, P], F32R, at_mix)
        p_lo = sb("p_lo", [P, PAGES, P], F32R, at_mix)
        p_new = sb("p_new", [NQ, P], F32, at_mix)
        v_new = sb("v_new", [NQ, HEADS * DV], F32, at_mix)
        s_all = sb("s_all", [P, PAST + NQ], F32, at_mix)
        o_rows = sb("o_rows", [P, HEADS * DV], F32, at_mix)
        o_second = sb("o_second", [P, HEADS, NQ], F32, at_mix)
        q_all = sb("q_all", [P, 8, NB * NQ], F32, at_mix)
        near = sb("near", [P, NEAR], F32, at_mix)
        s_n = sb("s_n", [P, NQ], F32, at_mix)
        far = sb("far", [P, 2], F32, at_mix)
        mxk = sb("mxk", [P, 6], F32, at_mix)
        l_all = sb("l_all", [P, 2], F32, at_mix)
        w_row = sb("w_row", [P, 1], F32, at_mix)
        pages = sb("pages", [1, NB * PAGES], I32, at_mix)
        at_mix.close()

        at_branch = ExitStack()
        sb("below_branch", [P, 4, T], F32, at_branch)
        br_hi = [sb(f"br_hi{b}", [P, HEADS, T], F32R, at_branch) for b in range(2)]
        br_lo = [sb(f"br_lo{b}", [P, HEADS, T], F32R, at_branch) for b in range(2)]
        m_hi = sb("m_hi", [P, KT, T], F32R, at_branch)
        m_lo = sb("m_lo", [P, KT, T], F32R, at_branch)
        gates = sb("gates", [P, 2, 4, T], F32, at_branch)
        at_branch.close()
        at_end = ExitStack()
        sb("below_end", [P, 4, T], F32, at_end)
        ffn = sb("ffn", [P, KT, T], F32, at_end)
        hid_hi = [sb(f"hid_hi{j}", [P, T], F32R, at_end) for j in range(HALVES)]
        hid_lo = [sb(f"hid_lo{j}", [P, T], F32R, at_end) for j in range(HALVES)]
        sb("below_y_tok", [P, 8, T], F32, at_end)
        y_tok = sb("y_tok", [P, 3, D_MODEL], F32, at_end)
        at_end.close()
        sq_sum, sq_part, rs_mix, rs_ffn = (sb(n, [P, T]) for n in ("sq_sum", "sq_part", "rs_mix", "rs_ffn"))
        h2_hi = sb("h2_hi", [P, KT, T], F32R)
        h2_lo = sb("h2_lo", [P, KT, T], F32R)
        at_out = ExitStack()
        sb("below_mixed", [P, 2 * KT, T], F32, at_out)
        mixed = sb("mixed", [P, KT, T], F32, at_out)
        at_out.close()
        hidden = sb("hidden", [P, FT_N, T])
        n_sq, n_gate, n_rs, n_e = (stage[0][:, m, :] for m in range(4))

        raw_landed = [sem(f"raw_landed{j}") for j in range(RAW)]
        hi_ready = sem("hi_ready")
        lo_ready = sem("lo_ready")
        granule_used = sem("granule_used")
        set_done = sem("set_done")
        set_out = sem("set_out")
        stage_free = sem("stage_free")
        u_stored = sem("u_stored")
        const_landed = sem("const_landed")
        const_ready = sem("const_ready")

        x_landed = [sem(f"x_landed{j}") for j in range(3)]
        tiles = range(KT)
        u_pe = Steps(sem("u_pe"), "bias rs " + " ".join(f"x{g}" for g in tiles))
        u_act = Steps(sem("u_act"), "sq0 sq1 sq2 root lb_e lam_e " + " ".join(f"x{g} h{g}" for g in tiles))
        u_vec = Steps(sem("u_vec"), "ones tab lb_max lb_d lam_p lam_d rs_inv rsb bias_vec rs "
                      + " ".join(f"h{g} l{g}" for g in tiles) + " lb_s lb_r lb omlb aT lam1 lam2 neg cf")
        u_pool = Steps(sem("u_pool"), "zero mean")
        x_kept = [sem(f"x_kept{j}") for j in range(2)]
        bias_stored = sem("bias_stored")
        head_landed = [sem(f"head_landed{j}") for j in range(2)]
        HEAD_LOADS = 16 * 9
        h_pe = Steps(sem("h_pe"), "scores vk i_t kd_t a ds pd_t pv ds_s o", 2)
        h_act = Steps(sem("h_act"), "ef lg eG tok p i_tok kd_tok pdt o_att", 2)
        h_vec = Steps(sem("h_vec"), "sg1 sg fg kin G Gd s max nmax qkd rc rcl pd2 pd own aT st1 st2 st3 st4 s_new o", 2)
        passed = sem("passed")
        h_pool = Steps(sem("h_pool"), "stored", 2)
        head_stored = sem("head_stored")
        k_turned, v_used = sem("k_turned"), sem("v_used")
        mix_landed, pages_landed = sem("mix_landed"), sem("pages_landed")
        s_n_landed, gate_landed, v_n_landed = sem("s_n_landed"), sem("gate_landed"), sem("v_n_landed")
        k_pe = Steps(sem("k_pe"), "ss s0 s1 s2 s3", 1)
        k_act = Steps(sem("k_act"), "q sq rt g0 g1 g2 g3 p", 1)
        k_vec = Steps(sem("k_vec"), "q rs e1 e2 e3 on og m0 m1 m2 near m3 mx nmx r w", 1)
        v_pe = Steps(sem("v_pe"), "t0 t1 new ot", 1)
        v_act = Steps(sem("v_act"), "h0 h1 o ot", 1)
        v_vec = Steps(sem("v_vec"), "l0 l1 o", 1)
        q_zero = sem("q_zero")
        d_pe = Steps(sem("d_pe"), "ss0 ss1")
        d_act = Steps(sem("d_act"), "hh sq0 sq1 rt0 rt1 dh")
        d_vec = Steps(sem("d_vec"), "hl r0 n0 r1 n1 dl")
        b_act = Steps(sem("b_act"), "e hi")
        b_vec = Steps(sem("b_vec"), "one inv yh yd sum lo")
        gates_landed, x_back = sem("gates_landed"), sem("x_back")
        m_act = Steps(sem("m_act"), "copy sq", 2)
        m_vec = Steps(sem("m_vec"), "part sum", 2)
        e_pe = Steps(sem("e_pe"), "ss")
        e_act = Steps(sem("e_act"), "rt h0 sq0 h1 sq1 h2 sq2 h3 sq3 rt2")
        e_vec = Steps(sem("e_vec"), "rs n0 x0 l0 p0 s0 n1 x1 l1 p1 s1 n2 x2 l2 p2 s2 n3 x3 l3 p3 s3 rs2")
        e_pe2 = Steps(sem("e_pe2"), "ss")
        f_act = Steps(sem("f_act"), "e")
        f_vec = Steps(sem("f_vec"), "g one inv gs u act")
        down_done = sem("down_done")
        g_act = Steps(sem("g_act"), "c0 c1 c2 c3 c4 c5 c6 c7 q0 q1")
        g_vec = Steps(sem("g_vec"), "p0 s0 p1 s1")
        y_pe = Steps(sem("y_pe"), "ss " + " ".join(f"t{k}" for k in range(12)))
        y_act = Steps(sem("y_act"), "rt " + " ".join(f"o{k}" for k in range(12)))
        y_vec = Steps(sem("y_vec"), "rs n0 y0 n1 y1 n2 y2 n3 y3")
        sums_zero = sem("sums_zero")
        y_stored = sem("y_stored")
        block = ctx.enter_context(nc.Block())

        def w_granule(w, q, n):
            return w.rearrange("(q c p) n -> q p c n", c=2, p=P)[q][:, :, bass.ds(n * 512, 512)]

        def load(sp, r, slot, src, first=False):
            if not first:
                sp.wait_ge(lo_ready, r - RAW + 1)
            dst = raw[slot][:, :]
            if len(src.shape) == 3:
                dst = dst.rearrange("p (c n) -> p c n", c=2)
            sp.dma_start(dst, src).then_inc(raw_landed[slot], 16)

        def split_hi(act, r, slot, use, first=False):
            act.wait_ge(raw_landed[slot], 16 * use)
            if not first:
                act.wait_ge(granule_used, r - HALVES + 1)
            act.activation(w_hi[slot % HALVES][:, :], raw[slot][:, :], ACT.Copy).then_inc(hi_ready, 1)

        def split_lo(dve, r, slot):
            dve.wait_ge(hi_ready, r + 1)
            dve.tensor_tensor(w_lo[slot % HALVES][:, :], raw[slot][:, :],
                              w_hi[slot % HALVES][:, :].bitcast(F32), ALU.subtract).then_inc(lo_ready, 1)

        def products(pe, r, slot, xh, xl, bank, q, nq, free, by_bank=True):
            pe.wait_ge(lo_ready, r + 1)
            wh = w_hi[slot % HALVES][:, :].rearrange("p (c m k) -> p c m k", c=2, m=4)
            wl = w_lo[slot % HALVES][:, :].rearrange("p (c m k) -> p c m k", c=2, m=4)
            for m in range(4):
                if q == 0:
                    free(m)
                out = ps[:, bank + m, 0:T]
                for c in range(2):
                    first, last = q == 0 and c == 0, q == nq - 1 and c == 1
                    pe.matmul(out, wh[:, c, m, :], xh(c), start=first, stop=False)
                    pe.matmul(out, wl[:, c, m, :], xh(c), start=False, stop=False)
                    mm = pe.matmul(out, wh[:, c, m, :], xl(c), start=False, stop=last)
                if by_bank and q == nq - 1 and m < 3:
                    mm.then_inc(set_done, 1)
            mm.then_inc(granule_used, 1)

        def bank_ready(eng, s, m, r_end):
            if m < 3:
                eng.wait_ge(set_done, 3 * s + m + 1)
            else:
                eng.wait_ge(granule_used, r_end)

        NT = [(0, P), (P, P), (2 * P, CHUNK)]

        CONSTS = 16 * 11

        def head_loads(sp, h, par):
            sp.wait_ge(u_stored, 16 * (SETS_HEAD - 1) + 16 * h)
            sp.wait_ge(h_pe.sem, h_pe.last(h - 2))
            sp.wait_ge(h_vec.sem, h_vec.last(h - 2))
            sp.wait_ge(bias_stored, 16)
            sp.wait_ge(u_act.sem, u_act.last(0))
            sp.wait_ge(u_vec.sem, u_vec.last(0))
            for j in range(2):
                sp.wait_ge(x_kept[j], 32)
            done = head_landed[par]
            sp.dma_start(hin[par][:, :, :], uT[0:24].rearrange("(c h) p t -> h p c t", c=3)[
                bass.ds(h, 1)].rearrange("a p c t -> (a p) c t")).then_inc(done, 16)
            for dst, tile in ((mq, DQT), (mk, DKT)):
                rows = uT[tile:tile + 8].rearrange("(m c) (e d) t -> m (c e) d t", m=2, e=2)
                for m in range(2):
                    sp.dma_start(dst[par][DH * m:DH * m + DH, :],
                                 rows[m][bass.ds(h, 1)].rearrange("a d t -> (a d) t")).then_inc(done, 16)
            sp.dma_start(mv[par][:, :], uT[bass.ds(DVT + h, 1)].rearrange("a p t -> (a p) t")).then_inc(done, 16)
            sp.dma_start(s0[par][:, :, :], st.rearrange("b h p v -> h p b v")[
                bass.ds(h, 1)].rearrange("a p b v -> (a p) b v")).then_inc(done, 16)
            for m in range(2):
                skew = bass.AP(bias_rows.tensor, (h + 8 * m) * (P * BIAS_L) + P - 1,
                               [[BIAS_L - 1, P], [1, 2 * P]])
                sp.dma_start(mb[par][:, m, :], skew).then_inc(done, 16)

        def read_set(act, s, r_end, to):
            act.wait_ge(stage_free, s + 1)
            for m in range(4):
                bank_ready(act, s, m, r_end)
                act.activation(stage[to][:, m, :], ps[:, m, 0:T], ACT.Copy).then_inc(set_out, 1)

        def act_block(act, n, par, head=None):
            for q in range(8):
                split_hi(act, 8 * n + q, q, n + 1)
                if head and q != 1:
                    act_head(act, q, par, *head)
                if q == 1:
                    read_set(act, n - 1, 8 * n, 1 - par)
                    if head:
                        act_head(act, q, par, *head)

        def act_head(act, q, par, h, i):
            x = hin[par]
            if q == 0:
                h_act.begin()
                act.wait_ge(head_landed[par], HEAD_LOADS * (i + 1))
                act.wait_ge(h_vec.sem, h_vec.last(h - 1))
                act.wait_ge(h_pe.sem, h_pe.last(h - 1))
                act.wait_ge(h_pool.sem, h_pool.last(h - 1))
                act.wait_ge(h_act.sem, h_act.last(h - 1))
                h_act.done(act.activation(kin[:, :], x[:, 1, :], ACT.Exp, scale=-1.0), "ef")
            if q == 1:
                act.wait_ge(h_vec.sem, h_vec.at(h, "fg"))
                h_act.done(act.activation(lg[:, :], fg[:, :], ACT.Ln), "lg")
            if q == 2:
                act.wait_ge(h_vec.sem, h_vec.at(h, "Gd"))
                act.activation(eG[:, :], G[:, :], ACT.Exp)
                act.activation(kg[:, :], G[:, :], ACT.Exp, scale=-1.0)
                h_act.done(act.activation(kd[:, :], lg[:, :], ACT.Exp), "eG")
                act.wait_ge(h_pe.sem, h_pe.at(h, "vk"))
                for bank, dst in ((6, v_tok), (7, k_tok)):
                    act.activation(dst[:, 0:2, :], ps[:, bank, 0:2 * P].rearrange("p (c d) -> p c d", c=2), ACT.Copy)
                    ins = act.activation(dst[0:CHUNK, 2, :], ps[0:CHUNK, bank, 2 * P:3 * P], ACT.Copy)
                h_act.done(ins, "tok")
            if q == 3:
                act.wait_ge(h_vec.sem, h_vec.at(h, "nmax"))
                for m in range(2):
                    for b, (c0, c1) in enumerate(((0, P), (P, 3 * P))):
                        k = 2 * m + b
                        ins = act.activation(s_at[:, m, c0:c1], s_at[:, m, c0:c1], ACT.Exp,
                                             bias=nmx[:, k:k + 1], accum_out=sm[:, k:k + 1])
                h_act.done(ins, "p")
                act.wait_ge(h_pe.sem, h_pe.at(h, "i_t"))
                act.activation(i_tok[:, 0:4, :], ps[0:CHUNK, 6, :].rearrange("p (c d) -> p c d", c=4), ACT.Copy)
                h_act.done(act.activation(i_tok[:, 4, :], ps[0:CHUNK, 7, 0:P], ACT.Copy), "i_tok")
            if q == 5:
                act.wait_ge(h_pe.sem, h_pe.at(h, "kd_t"))
                act.activation(kd_tok[:, 0:4, :], ps[0:CHUNK, 4, :].rearrange("p (c d) -> p c d", c=4), ACT.Copy)
                h_act.done(act.activation(kd_tok[:, 4, :], ps[0:CHUNK, 7, P:2 * P], ACT.Copy), "kd_tok")
            if q == 6:
                act.wait_ge(h_pe.sem, h_pe.at(h, "pd_t"))
                h_act.done(act.activation(pdt[:, :, :], ps[:, 6, 0:3 * P].rearrange("p (c d) -> p c d", c=3),
                                          ACT.Copy), "pdt")
            if q == 7:
                act.wait_ge(h_pe.sem, h_pe.at(h, "pv"))
                h_act.done(act.activation(o_da[:, bass.ds(h, 1), 0:SEQ].rearrange("p a t -> p (a t)"),
                                          ps[:, 5, 0:SEQ], ACT.Copy), "o_att")

        def vec_head(dve, q, par, h, i):
            def chain(ins, name):
                h_vec.done(ins, name)
                dve.wait_ge(h_vec.sem, h_vec.at(h, name))

            x = hin[par]
            if q == 0:
                h_vec.begin()
                dve.wait_ge(h_act.sem, h_act.at(h, "ef"))
                chain(dve.tensor_scalar(kin[:, :], kin[:, :], 1.0, None, ALU.add), "sg1")
                chain(dve.reciprocal(kin[:, :], kin[:, :]), "sg")
                chain(dve.tensor_scalar(fg[:, :], kin[:, :], omlb[:, bass.ds(h, 1)], lb[:, bass.ds(h, 1)],
                                        ALU.mult, ALU.add), "fg")
                h_vec.done(dve.tensor_scalar(kin[:, :], fg[:, :], -1.0, 1.0, ALU.mult, ALU.add), "kin")
            if q == 1:
                dve.wait_ge(h_act.sem, h_act.at(h, "lg"))
                chain(dve.tensor_tensor_scan(G[:, :], scan_keep[:, :], lg[:, :], 0.0, ALU.mult, ALU.add), "G")
                for t0, k, n in ((0, SEQ // CHUNK, CHUNK), (SEQ, NB, NQ)):
                    g = G[:, t0:t0 + k * n].rearrange("p (k n) -> p k n", n=n)
                    ins = dve.tensor_tensor(lg[:, t0:t0 + k * n].rearrange("p (k n) -> p k n", n=n),
                                            g[:, :, n - 1:n].broadcast_to([P, k, n]), g, ALU.subtract)
                h_vec.done(ins, "Gd")
            if q == 2:
                dve.wait_ge(h_pe.sem, h_pe.at(h, "scores"))
                for m in range(2):
                    near = mb[par][:, m, :]
                    dve.scalar_tensor_tensor(s_at[:, m, 0:P], ps[:, 4 + m, 0:P], SCALE, near[:, P:2 * P],
                                             ALU.mult, ALU.add)
                    dve.scalar_tensor_tensor(s_at[:, m, P:3 * P], ps[:, 4 + m, P:3 * P], SCALE, near,
                                             ALU.mult, ALU.add)
                    ins = dve.tensor_scalar(s_sm[:, m, :], ps[0:CHUNK, 4 + m, 3 * P:3 * P + CHUNK], SCALE,
                                            None, ALU.mult)
                chain(ins, "s")
                for m in range(2):
                    dve.tensor_reduce(mx[:, 2 * m:2 * m + 1], s_at[:, m, 0:P], AX_X, ALU.max)
                    ins = dve.tensor_reduce(mx[:, 2 * m + 1:2 * m + 2], s_at[:, m, P:3 * P], AX_X, ALU.max)
                chain(ins, "max")
                h_vec.done(dve.tensor_scalar(nmx[:, :], mx[:, :], -1.0, None, ALU.mult), "nmax")
            if q == 3:
                dve.wait_ge(h_act.sem, h_act.at(h, "eG"))
                dve.tensor_tensor(qg[:, :], x[:, 0, :], eG[:, :], ALU.mult)
                dve.tensor_tensor(kg[:, :], kg[:, :], kin[:, :], ALU.mult)
                h_vec.done(dve.tensor_tensor(kd[:, :], kd[:, :], kin[:, :], ALU.mult), "qkd")
            if q == 4:
                dve.wait_ge(h_act.sem, h_act.at(h, "p"))
                chain(dve.reciprocal(rc[:, :], sm[:, :]), "rc")
                chain(dve.tensor_scalar(rc[:, 2:4], rc[:, 2:4], neg_lam[:, 0:1], None, ALU.mult), "rcl")
                spans = ((0, P), (P, 3 * P))
                for b, (c0, c1) in enumerate(spans):
                    ins = dve.tensor_scalar(pd2[:, c0:c1], s_at[:, 1, c0:c1], rc[:, 2 + b:3 + b], None, ALU.mult)
                chain(ins, "pd2")
                for b, (c0, c1) in enumerate(spans):
                    ins = dve.scalar_tensor_tensor(pd[:, c0:c1], s_at[:, 0, c0:c1], rc[:, b:b + 1],
                                                   pd2[:, c0:c1], ALU.mult, ALU.add)
                h_vec.done(ins, "pd")
            if q == 5:
                dve.wait_ge(h_act.sem, h_act.at(h, "i_tok"))
                h_vec.done(dve.tensor_tensor(
                    i_own[:, :, :], i_tok[:, 4:5, :].broadcast_to([CHUNK, NB, DV]),
                    own[:, :].unsqueeze(2).broadcast_to([CHUNK, NB, DV]), ALU.mult), "own")
                dve.wait_ge(h_pe.sem, h_pe.at(h, "a"))
                dve.sem_inc(passed, 1)
                h_vec.done(dve.copy_predicated(aT[:, :, :].rearrange("p c n -> p (c n)"),
                                               causal[:, :, :].rearrange("p c n -> p (c n)"),
                                               ps[0:CHUNK, 5, 0:T]), "aT")
            if q == 6:
                dve.wait_ge(h_pe.sem, h_pe.at(h, "ds"))
                chain(dve.tensor_copy(state[:, 0, :], ps[:, 4, 0:DV]), "st1")
                for c in range(1, 4):
                    last = CHUNK * c + CHUNK - 1
                    ins = dve.scalar_tensor_tensor(state[:, c, :], state[:, c - 1, :], eG[:, last:last + 1],
                                                   ps[:, 4, c * DV:(c + 1) * DV], ALU.mult, ALU.add)
                    chain(ins, f"st{c + 1}")
            if q == 7:
                dve.wait_ge(h_pe.sem, h_pe.at(h, "ds_s"))
                for b in range(NB):
                    last = SEQ + NQ * b + NQ - 1
                    ins = dve.scalar_tensor_tensor(s_new[:, b, :], s0[par][:, b, :], eG[:, last:last + 1],
                                                   ps[:, 6 + b // 4, b % 4 * DV:(b % 4 + 1) * DV],
                                                   ALU.mult, ALU.add)
                h_vec.done(ins, "s_new")
                dve.wait_ge(h_pe.sem, h_pe.at(h, "o"))
                h_vec.done(dve.tensor_copy(o_hg[:, bass.ds(h, 1), :].rearrange("p a t -> p (a t)"),
                                           ps[:, 4, 0:T]), "o")

        def pe_head(pe, q, par, h, i):
            x, seq = hin[par], range(SEQ // CHUNK)
            span = [slice(CHUNK * c, CHUNK * (c + 1)) for c in range(CHUNKS)]

            def five(src, bank, col):
                pe.sem_inc(passed, 1)
                for c in range(CHUNKS):
                    out = ps[0:CHUNK, bank, c * P:(c + 1) * P] if c < 4 else ps[0:CHUNK, 7, col:col + P]
                    ins = pe.transpose(out, src[:, span[c]], ident[:, :])
                return ins

            if q == 0:
                h_pe.begin()
                pe.wait_ge(head_landed[par], HEAD_LOADS * (i + 1))
                pe.wait_ge(h_act.sem, h_act.last(h - 1))
                pe.wait_ge(h_vec.sem, h_vec.last(h - 1))
                for m in range(2):
                    own_q, own_k = mq[par][DH * m:DH * m + DH, :], mk[par][DH * m:DH * m + DH, :]
                    pe.matmul(ps[:, 4 + m, 0:P], own_q[:, 0:P], own_k[:, 0:P], start=True, stop=True)
                    pe.matmul(ps[:, 4 + m, P:3 * P], own_q[:, P:SEQ], own_k[:, 0:SEQ], start=True, stop=True)
                    ins = pe.matmul(ps[0:CHUNK, 4 + m, 3 * P:3 * P + CHUNK], own_q[:, SEQ:T], own_k[:, SEQ:T],
                                    start=True, stop=True)
                h_pe.done(ins, "scores")
                for bank, src in ((6, mv), (7, mk)):
                    for j, (t0, n) in enumerate(NT):
                        ins = pe.transpose(ps[0:n, bank, j * P:(j + 1) * P], src[par][:, t0:t0 + n], ident[:, :])
                h_pe.done(ins, "vk")
            if q == 1:
                pe.wait_ge(h_act.sem, h_act.at(h, "tok"))
                h_pe.done(five(x[:, 2, :], 6, 0), "i_t")
            if q == 3:
                pe.wait_ge(h_vec.sem, h_vec.at(h, "qkd"))
                pe.wait_ge(h_act.sem, h_act.at(h, "i_tok"))
                h_pe.done(five(kd, 4, P), "kd_t")
                for c in range(CHUNKS):
                    ins = pe.matmul(ps[0:CHUNK, 5, span[c]], kg[:, span[c]], qg[:, span[c]], start=True, stop=True)
                h_pe.done(ins, "a")
            if q == 4:
                pe.wait_ge(h_act.sem, h_act.at(h, "kd_tok"))
                for c in seq:
                    ins = pe.matmul(ps[:, 4, c * DV:(c + 1) * DV], kd_tok[:, c, :], i_tok[:, c, :],
                                    start=True, stop=True)
                h_pe.done(ins, "ds")
                pe.wait_ge(h_vec.sem, h_vec.at(h, "pd"))
                for j in range(3):
                    ins = pe.transpose(ps[:, 6, j * P:(j + 1) * P], pd[:, j * P:(j + 1) * P], ident[:, :])
                h_pe.done(ins, "pd_t")
            if q == 5:
                pe.wait_ge(h_act.sem, h_act.at(h, "pdt"))
                pe.wait_ge(h_vec.sem, h_vec.at(h, "aT"))
                pe.matmul(ps[:, 5, 0:P], v_tok[:, 0, :], pdt[:, 0, :], start=True, stop=True)
                pe.matmul(ps[:, 5, P:2 * P], v_tok[:, 0, :], pdt[:, 1, :], start=True, stop=False)
                h_pe.done(pe.matmul(ps[:, 5, P:2 * P], v_tok[:, 1, :], pdt[:, 2, :], start=False, stop=True), "pv")
                for k in range(2):
                    ins = pe.matmul(ps[:, 6 + k, :], kd_tok[:, 4, :], i_own[:, 4 * k:4 * k + 4, :],
                                    start=True, stop=True)
                h_pe.done(ins, "ds_s")
            if q == 6:
                pe.wait_ge(h_vec.sem, h_vec.at(h, "st4"))
                for c in seq:
                    pe.matmul(ps[:, 4, span[c]], i_tok[:, c, :], aT[:, c, :], start=True, stop=c == 0)
                    if c:
                        pe.matmul(ps[:, 4, span[c]], state[:, c - 1, :], qg[:, span[c]], start=False, stop=True)
                pe.matmul(ps[:, 4, span[4]], i_tok[:, 4, :], aT[:, 4, :], start=True, stop=True)
                for b in range(NB):
                    t0 = SEQ + NQ * b
                    ins = pe.matmul(ps[:, 4, t0:t0 + NQ], s0[par][:, b, :], qg[:, t0:t0 + NQ],
                                    start=False, stop=True, skip_group_check=True)
                h_pe.done(ins, "o")

        def store_set(pool, s, at):
            pool.wait_ge(set_out, 4 * s + 4)
            pool.dma_start(uT[bass.ds(4 * s, 4)].rearrange("c p t -> p c t"), stage[at][:, :, :]).then_inc(u_stored, 16)
            pool.wait_ge(u_stored, 16 * s + 16)
            pool.sem_inc(stage_free, 1)

        HEAD_STORES = 16 * 9

        def pool_head(pool, par, h):
            def two(a):
                return a.rearrange("(c p) d -> p c d", p=P)

            one = bass.ds(h, 1)
            pool.wait_ge(h_act.sem, h_act.at(h, "tok"))
            kp = k_p.rearrange("t (m h) d -> m h t d", m=2)
            ks = k_s.rearrange("t (m h) d -> m h t d", m=2)
            for m in range(2):
                c = slice(DH * m, DH * m + DH)
                pool.dma_start(two(kp[m][one].rearrange("a t d -> (a t) d")), k_tok[:, 0:2, c]).then_inc(head_stored, 16)
                pool.dma_start(ks[m][one].rearrange("a t d -> (a t) d"), k_tok[0:CHUNK, 2, c]).then_inc(head_stored, 16)
            pool.dma_start(two(v_p.rearrange("t h d -> h t d")[one].rearrange("a t d -> (a t) d")),
                           v_tok[:, 0:2, :]).then_inc(head_stored, 16)
            pool.dma_start(v_s.rearrange("t h d -> h t d")[one].rearrange("a t d -> (a t) d"),
                           v_tok[0:CHUNK, 2, :]).then_inc(head_stored, 16)
            pool.wait_ge(h_vec.sem, h_vec.at(h, "s"))
            pool.dma_start(new_scores.rearrange("(m h) q k -> h q m k", m=2)[one].rearrange("a q m k -> (a q) m k"),
                           s_sm[:, :, :]).then_inc(head_stored, 16)
            pool.wait_ge(h_vec.sem, h_vec.at(h, "s_new"))
            pool.dma_start(h_p[one].rearrange("a p v -> (a p) v"), state[:, 3, :]).then_inc(head_stored, 16)
            pool.dma_start(h_s.rearrange("b h p v -> h p b v")[one].rearrange("a p b v -> (a p) b v"),
                           s_new[:, :, :]).then_inc(head_stored, 16)
            pool.wait_ge(head_stored, HEAD_STORES * (h + 1))
            pool.sem_inc(h_pool.sem, 1)

        def order(has_k, has_v):
            if not (has_k and has_v):
                return [("K" if has_k else "V", p) for p in range(PAGES)]
            out = [("K", p) for p in range(4)]
            for p in range(4, PAGES):
                out += [("V", p - 4), ("K", p)]
            return out + [("V", p) for p in range(PAGES - 4, PAGES)]

        def mix_r(n, has_k, has_v, what):
            at = order(has_k, has_v).index(what)
            past = 0 if not has_v else PAGES + 2 * PAGES * (n - 1)
            use = R_MIX // RAW + (0 if not has_v else PAGES // RAW + 2 * PAGES // RAW * (n - 1))
            return R_MIX + past + at, at % RAW, use + at // RAW + 1

        def rounds(eng, do):
            do(eng, 0, True, False)
            with eng.Fori(1, NB) as n:
                do(eng, n, True, True)
            do(eng, NB, False, True)

        def heads_of(t, d, step):
            return bass.AP(t.tensor, t.offset + d, [list(t.ap[0]), [step, 8], [1, NQ]])

        def sync_mix(sp, n, has_k, has_v):
            if not has_v:
                sp.wait_ge(pages_landed, 16)
            for kind, p in order(has_k, has_v):
                r, slot, _ = mix_r(n, has_k, has_v, (kind, p))
                cache, b = (ck, n) if kind == "K" else (cv, n - 1)
                page = sp.value_load(pages[0:1, bass.ds(b * PAGES + p, 1)], min_val=0, max_val=POOL - 1)
                load(sp, r, slot, cache[bass.ds(page, 1)].rearrange("a p n -> (a p) n"))

        def turned(t, p):
            return t[p // 4 % 2][:, :, p % 4 * PAGE:(p % 4 + 1) * PAGE]

        def bank_pair(p):
            return ps[:, p % 2 * 2:p % 2 * 2 + 2, :].rearrange("p b n -> p (b n)").rearrange(
                "p (c k) -> p c k", c=8)

        def act_mix(act, n, has_k, has_v):
            b = n - 1
            k_act.begin()
            v_act.begin()

            def value_hi(j):
                r, slot, use = mix_r(n, has_k, has_v, ("V", j))
                act.wait_ge(raw_landed[slot], 16 * use)
                act.wait_ge(v_used, PAGES * b + j + 1)
                act.activation(w_hi[slot % HALVES][:, :], raw[slot][:, :], ACT.Copy).then_inc(hi_ready, 1)

            def group(g):
                act.wait_ge(k_pe.sem, k_pe.at(n, f"s{g}"))
                w = 4 * PAGE if g < 3 else 3 * PAGE
                k_act.done(act.activation(s_all[:, g * 4 * PAGE:g * 4 * PAGE + w], ps[:, 4 + g % 2, 0:w],
                                          ACT.Identity, bias=far[:, 0:1]), f"g{g}")

            if has_k:
                act.wait_ge(k_pe.sem, k_pe.at(n - 1, "s3"))
                act.wait_ge(k_vec.sem, k_vec.at(n - 1, "w"))
                act.wait_ge(mix_landed, MIX_LOADS)
                for m in range(2):
                    own = slice(DH * m, DH * m + DH)
                    ins = act.activation(heads_of(q_hi[own, :, :], NQ * m, P + 2 * NQ),
                                         q_all[own, :, bass.ds(NQ * n, NQ)], ACT.Copy, scale=SCALE)
                k_act.done(ins, "q")
                k_act.done(act.activation(n_sq, o_hg[:, bass.ds(n, 1), :].rearrange("p a t -> p (a t)"),
                                          ACT.Square), "sq")
            for p in range(PAGES):
                if has_v and p in (2, 3):
                    j = p - 2
                    act.wait_ge(v_pe.sem, v_pe.at(b, f"t{j}"))
                    ins = act.activation(p_hi[:, 8 * j:8 * j + 8, :], ps[:, 4:6, :].rearrange(
                        "p b n -> p (b n)").rearrange("p (c k) -> p c k", c=8), ACT.Copy)
                    if j:
                        ins = act.activation(p_new[:, :], ps[0:NQ, 6, 0:P], ACT.Copy)
                    v_act.done(ins, f"h{j}")
                if has_v and p >= 4:
                    value_hi(p - 4)
                if has_k:
                    r, _, _ = mix_r(n, has_k, has_v, ("K", p))
                    act.wait_ge(k_turned, PAGES * n + p + 1)
                    act.activation(turned(kt_hi, p), bank_pair(p), ACT.Copy).then_inc(hi_ready, 1)
                    if p == 1:
                        act.wait_ge(k_pe.sem, k_pe.at(n, "ss"))
                        act.wait_ge(gate_landed, 16 * (n + 1))
                        act.activation(n_rs, ps[:, 7, 0:T], ACT.Sqrt, scale=1.0 / DV, bias=eps_c[:, 0:1])
                        k_act.done(act.activation(n_e, n_gate, ACT.Exp, scale=-1.0), "rt")
                    if p in (5, 9, 13):
                        group((p - 5) // 4)
            if has_v:
                value_hi(PAGES - 4)
                value_hi(PAGES - 3)
            if has_k:
                group(3)
            if has_v:
                value_hi(PAGES - 2)
                value_hi(PAGES - 1)
            if has_k:
                act.wait_ge(k_vec.sem, k_vec.at(n, "nmx"))
                k_act.done(act.activation(s_all[:, :], s_all[:, :], ACT.Exp, bias=mxk[:, 5:6],
                                          accum_out=l_all[:, 0:1]), "p")
            if has_v:
                act.wait_ge(v_pe.sem, v_pe.at(b, "new"))
                v_act.done(act.activation(o_rows[:, :], ps[:, 6:8, :].rearrange("p b n -> p (b n)"),
                                          ACT.Copy, scale=w_row[:, 0:1]), "o")
                act.wait_ge(v_pe.sem, v_pe.at(b, "ot"))
                v_act.done(act.activation(o_second[:, :, :], heads_of(ps[:, 4:6, :], 64, P + NQ), ACT.Copy), "ot")

        def vec_mix(dve, n, has_k, has_v):
            b = n - 1
            k_vec.begin()
            v_vec.begin()

            def chain(ins, name):
                k_vec.done(ins, name)
                dve.wait_ge(k_vec.sem, k_vec.at(n, name))

            def value_lo(j):
                r, slot, _ = mix_r(n, has_k, has_v, ("V", j))
                split_lo(dve, r, slot)

            if has_k:
                dve.wait_ge(k_act.sem, k_act.at(n, "q"))
                for m in range(2):
                    own = slice(DH * m, DH * m + DH)
                    ins = dve.scalar_tensor_tensor(
                        heads_of(q_lo[own, :, :], NQ * m, P + 2 * NQ), q_all[own, :, bass.ds(NQ * n, NQ)],
                        SCALE, heads_of(q_hi[own, :, :].bitcast(F32), NQ * m, P + 2 * NQ), ALU.mult, ALU.subtract)
                k_vec.done(ins, "q")
            for p in range(PAGES):
                if has_v and p in (2, 3):
                    j = p - 2
                    dve.wait_ge(v_act.sem, v_act.at(b, f"h{j}"))
                    v_vec.done(dve.tensor_tensor(
                        p_lo[:, 8 * j:8 * j + 8, :],
                        ps[:, 4:6, :].rearrange("p b n -> p (b n)").rearrange("p (c k) -> p c k", c=8),
                        p_hi[:, 8 * j:8 * j + 8, :].bitcast(F32), ALU.subtract), f"l{j}")
                if has_v and p >= 4:
                    value_lo(p - 4)
                if has_k:
                    r, _, _ = mix_r(n, has_k, has_v, ("K", p))
                    dve.wait_ge(hi_ready, r + 1)
                    dve.tensor_tensor(turned(kt_lo, p), bank_pair(p), turned(kt_hi, p).bitcast(F32),
                                      ALU.subtract).then_inc(lo_ready, 1)
                    if p == 3:
                        o = o_hg[:, bass.ds(n, 1), :].rearrange("p a t -> p (a t)")
                        dve.wait_ge(k_act.sem, k_act.at(n, "rt"))
                        chain(dve.reciprocal(n_rs, n_rs), "rs")
                        chain(dve.tensor_scalar(n_e, n_e, 1.0, None, ALU.add), "e1")
                        chain(dve.reciprocal(n_e, n_e), "e2")
                        chain(dve.tensor_tensor(n_e, n_e, n_gate, ALU.mult), "e3")
                        chain(dve.scalar_tensor_tensor(o, o, hg_w[:, 0:1], n_rs, ALU.mult, ALU.mult), "on")
                        k_vec.done(dve.tensor_tensor(o, o, n_e, ALU.mult), "og")
                    if p in (5, 9, 13):
                        g = (p - 5) // 4
                        dve.wait_ge(k_act.sem, k_act.at(n, f"g{g}"))
                        k_vec.done(dve.tensor_reduce(mxk[:, g:g + 1], s_all[:, g * 4 * PAGE:(g + 1) * 4 * PAGE],
                                                     AX_X, ALU.max), f"m{g}")
            if has_v:
                value_lo(PAGES - 4)
                value_lo(PAGES - 3)
            if has_k:
                dve.wait_ge(k_act.sem, k_act.at(n, "g3"))
                dve.wait_ge(s_n_landed, 16 * (n + 1))
                dve.tensor_tensor(s_all[:, PAST - PAGE:PAST], ps[:, 5, 3 * PAGE:4 * PAGE], near[:, 0:PAGE], ALU.add)
                chain(dve.tensor_tensor(s_all[:, PAST:], s_n[:, :], near[:, PAGE:], ALU.add), "near")
                chain(dve.tensor_reduce(mxk[:, 3:4], s_all[:, 12 * PAGE:], AX_X, ALU.max), "m3")
                chain(dve.tensor_reduce(mxk[:, 4:5], mxk[:, 0:4], AX_X, ALU.max), "mx")
                k_vec.done(dve.tensor_scalar(mxk[:, 5:6], mxk[:, 4:5], -1.0, None, ALU.mult), "nmx")
            if has_v:
                value_lo(PAGES - 2)
                value_lo(PAGES - 1)
            if has_v:
                dve.wait_ge(v_act.sem, v_act.at(b, "ot"))
                v_vec.done(dve.tensor_tensor(o_da[:, :, bass.ds(SEQ + NQ * b, NQ)], o_second[:, :, :],
                                             heads_of(ps[:, 4:6, :], 0, P + NQ), ALU.add), "o")
            if has_k:
                dve.wait_ge(k_act.sem, k_act.at(n, "p"))
                chain(dve.reciprocal(l_all[:, 1:2], l_all[:, 0:1]), "r")
                k_vec.done(dve.tensor_tensor(w_row[:, :], l_all[:, 1:2], cf[:, :], ALU.mult), "w")

        def pe_mix(pe, n, has_k, has_v):
            b = n - 1
            k_pe.begin()
            v_pe.begin()

            def value(j):
                r, slot, _ = mix_r(n, has_k, has_v, ("V", j))
                pe.wait_ge(lo_ready, r + 1)
                if j == 0:
                    pe.wait_ge(v_vec.sem, v_vec.at(b, "l1"))
                wh, wl = w_hi[slot % HALVES], w_lo[slot % HALVES]
                for k in range(2):
                    c = slice(512 * k, 512 * k + 512)
                    pe.matmul(ps[:, 6 + k, :], p_hi[:, j, :], wh[:, c], start=j == 0, stop=False)
                    pe.matmul(ps[:, 6 + k, :], p_lo[:, j, :], wh[:, c], start=False, stop=False)
                    ins = pe.matmul(ps[:, 6 + k, :], p_hi[:, j, :], wl[:, c], start=False, stop=False)
                ins.then_inc(v_used, 1)

            def scores(g):
                r, _, _ = mix_r(n, has_k, has_v, ("K", 4 * g + 3))
                pe.wait_ge(lo_ready, r + 1)
                if g == 0:
                    pe.wait_ge(k_vec.sem, k_vec.at(n, "q"))
                    if has_v:
                        pe.wait_ge(v_vec.sem, v_vec.at(b, "l1"))
                if g >= 2:
                    pe.wait_ge(k_act.sem, k_act.at(n, f"g{g - 2}"))
                out, kh, kl = ps[:, 4 + g % 2, :], kt_hi[g % 2], kt_lo[g % 2]
                for c in range(8):
                    pe.matmul(out, q_hi[:, c, :], kh[:, c, :], start=c == 0, stop=False)
                    pe.matmul(out, q_lo[:, c, :], kh[:, c, :], start=False, stop=False)
                    ins = pe.matmul(out, q_hi[:, c, :], kl[:, c, :], start=False, stop=c == 7)
                k_pe.done(ins, f"s{g}")

            for p in range(PAGES):
                if has_k:
                    r, slot, use = mix_r(n, has_k, has_v, ("K", p))
                    pe.wait_ge(raw_landed[slot], 16 * use)
                    if p >= 2:
                        pe.wait_ge(lo_ready, mix_r(n, has_k, has_v, ("K", p - 2))[0] + 1)
                    else:
                        pe.wait_ge(lo_ready, mix_r(n, has_k, has_v, ("K", 0))[0])
                    for c in range(8):
                        ins = pe.transpose(bank_pair(p)[:, c, :], raw[slot][:, c * P:(c + 1) * P], ident[:, :])
                    ins.then_inc(k_turned, 1)
                    if p == 0:
                        pe.wait_ge(k_act.sem, k_act.at(n, "sq"))
                        if has_v:
                            pe.wait_ge(v_act.sem, v_act.at(b - 1, "ot"))
                        k_pe.done(pe.matmul(ps[:, 7, 0:T], ones[:, :], n_sq, start=True, stop=True), "ss")
                    if p >= 4 and p % 4 == 0:
                        scores(p // 4 - 1)
                if has_v and p in (2, 3):
                    j = p - 2
                    if j == 0:
                        pe.wait_ge(k_act.sem, k_act.at(b, "p"))
                        pe.wait_ge(v_vec.sem, v_vec.at(b - 1, "o"))
                    else:
                        pe.wait_ge(v_vec.sem, v_vec.at(b, "l0"))
                    for c in range(8):
                        t = 8 * j + c
                        ins = pe.transpose(ps[:, 4 + c // 4, c % 4 * P:(c % 4 + 1) * P],
                                           s_all[:, t * PAGE:(t + 1) * PAGE], ident[:, :])
                    if j:
                        ins = pe.transpose(ps[0:NQ, 6, 0:P], s_all[:, PAST:], ident[:, :])
                    v_pe.done(ins, f"t{j}")
                if has_v and p >= 4:
                    value(p - 4)
            if has_v:
                value(PAGES - 4)
            if has_k:
                scores(3)
            if has_v:
                for j in range(PAGES - 3, PAGES):
                    value(j)
                pe.wait_ge(v_n_landed, 16 * n)
                for k in range(2):
                    ins = pe.matmul(ps[:, 6 + k, :], p_new[:, :], v_new[:, 512 * k:512 * k + 512],
                                    start=False, stop=True)
                v_pe.done(ins, "new")
                pe.wait_ge(v_act.sem, v_act.at(b, "o"))
                if has_k:
                    pe.wait_ge(k_vec.sem, k_vec.at(n, "near"))
                for h in range(HEADS):
                    ins = pe.transpose(ps[:, 4 + h // 4, h % 4 * P:(h % 4 + 1) * P],
                                       o_rows[:, h * DV:(h + 1) * DV], ident[:, :])
                v_pe.done(ins, "ot")

        def pool_mix(pool, n, has_k, has_v):
            if has_k:
                pool.wait_ge(k_vec.sem, k_vec.at(n - 1, "near"))
                src = bass.AP(new_scores.tensor, (NB * NQ + 1) * NQ * n,
                              [[(NB * NQ) ** 2, MAPS], [NB * NQ, NQ], [1, NQ]])
                pool.dma_start(s_n[:, :], src).then_inc(s_n_landed, 16)
                pool.wait_ge(k_vec.sem, k_vec.at(n - 1, "og"))
                pool.dma_start(n_gate, uT[bass.ds(OT + n, 1)].rearrange("a p t -> (a p) t")).then_inc(gate_landed, 16)
            if has_v:
                pool.wait_ge(v_pe.sem, v_pe.at(n - 2, "new"))
                pool.dma_start(v_new[:, :], v_s.rearrange("(b q) h d -> b q (h d)", q=NQ)[
                    bass.ds(n - 1, 1)].rearrange("a q d -> (a q) d")).then_inc(v_n_landed, 16)

        MIX_LOADS = 16 * 3

        BLOCKS = D_MODEL // 512
        half = [slice(0, 4), slice(4, 8)]

        def branch_w(j, q):
            return w_granule(w_hg if q < 4 else w_da, q % 4, j)

        def act_branch(act, j, first=False):
            for q in range(8):
                r = R_BRANCH + 8 * j + q
                split_hi(act, r, q, r_use(R_BRANCH + q) + j)
                if first and q == 1:
                    for b in range(2):
                        act.wait_ge(d_pe.sem, d_pe.at(0, f"ss{b}"))
                        d_act.done(act.activation(stage[b][:, :, :], ps[:, 4:8, 0:T], ACT.Sqrt,
                                                  scale=1.0 / DV, bias=eps_c[:, 0:1]), f"rt{b}")
                if first and q == 2:
                    act.wait_ge(d_vec.sem, d_vec.at(0, "n1"))
                    for b in range(2):
                        ins = act.activation(br_hi[1][:, half[b], :], o_da[:, half[b], :], ACT.Copy,
                                             scale=1.0 - LAM_INIT)
                    d_act.done(ins, "dh")
                if not first and q == 2:
                    act_merged(act, j - 1)
                if q == 3:
                    b_act.begin()
                    act.wait_ge(gates_landed, 32 * (j + 1))
                    b_act.done(act.activation(gates[:, :, :, :], gates[:, :, :, :], ACT.Exp, scale=-1.0), "e")

        def act_merged(act, j):
            act.wait_ge(b_vec.sem, b_vec.at(j, "sum"))
            b_act.done(act.activation(m_hi[:, bass.ds(4 * j, 4), :], stage[0][:, :, :], ACT.Copy), "hi")

        def vec_branch(dve, j, first=False):
            def chain(ins, name, st=b_vec, rnd=j):
                st.done(ins, name)
                dve.wait_ge(st.sem, st.at(rnd, name))

            for q in range(8):
                r = R_BRANCH + 8 * j + q
                split_lo(dve, r, q)
                if first and q == 1:
                    for b in range(2):
                        dve.wait_ge(d_act.sem, d_act.at(0, f"rt{b}"))
                        chain(dve.reciprocal(stage[b][:, :, :], stage[b][:, :, :]), f"r{b}", d_vec, 0)
                        chain(dve.scalar_tensor_tensor(o_da[:, half[b], :], o_da[:, half[b], :], hg_w[:, 1:2],
                                                       stage[b][:, :, :], ALU.mult, ALU.mult), f"n{b}", d_vec, 0)
                if first and q == 2:
                    dve.wait_ge(d_act.sem, d_act.at(0, "dh"))
                    for b in range(2):
                        ins = dve.scalar_tensor_tensor(br_lo[1][:, half[b], :], o_da[:, half[b], :],
                                                       1.0 - LAM_INIT, br_hi[1][:, half[b], :].bitcast(F32),
                                                       ALU.mult, ALU.subtract)
                    chain(ins, "dl", d_vec, 0)
                if not first and q == 1:
                    vec_merge(dve, j - 1)
                if not first and q == 2:
                    vec_merged(dve, j - 1)
                if q == 4:
                    b_vec.begin()
                    dve.wait_ge(b_act.sem, b_act.at(j, "e"))
                    chain(dve.tensor_scalar(gates[:, :, :, :], gates[:, :, :, :], 1.0, None, ALU.add), "one")
                    chain(dve.reciprocal(gates[:, :, :, :], gates[:, :, :, :]), "inv")
                if q == 5:
                    dve.wait_ge(granule_used, R_BRANCH + 8 * j + 4)
                    if not first:
                        dve.wait_ge(b_vec.sem, b_vec.at(j - 1, "lo"))
                    b_vec.done(dve.tensor_tensor(stage[0][:, :, :], ps[:, 0:4, 0:T], gates[:, 0], ALU.mult), "yh")

        def vec_merge(dve, j):
            dve.wait_ge(granule_used, R_BRANCH + 8 * j + 8)
            b_vec.done(dve.tensor_tensor(stage[1][:, :, :], ps[:, 4:8, 0:T], gates[:, 1], ALU.mult), "yd")
            dve.wait_ge(b_vec.sem, b_vec.at(j, "yd"))
            b_vec.done(dve.tensor_tensor(stage[0][:, :, :], stage[0][:, :, :], stage[1][:, :, :], ALU.add), "sum")

        def vec_merged(dve, j):
            dve.wait_ge(b_act.sem, b_act.at(j, "hi"))
            b_vec.done(dve.tensor_tensor(m_lo[:, bass.ds(4 * j, 4), :], stage[0][:, :, :],
                                         m_hi[:, bass.ds(4 * j, 4), :].bitcast(F32), ALU.subtract), "lo")

        def pe_branch(pe, j, first=False):
            for q in range(8):
                r = R_BRANCH + 8 * j + q
                b = q // 4
                if first and q == 0:
                    pe.wait_ge(d_vec.sem, d_vec.at(0, "hl"))
                if first and q in (0, 2):
                    pe.wait_ge(d_act.sem, d_act.at(0, "sq1" if q == 0 else "rt0"))
                    for m in range(4):
                        ins = pe.matmul(ps[:, 4 + m, 0:T], ones[:, :], stage[q // 2][:, m, :], start=True, stop=True)
                    d_pe.done(ins, f"ss{q // 2}")
                if first and q == 4:
                    pe.wait_ge(d_vec.sem, d_vec.at(0, "dl"))

                def free(m):
                    if m == 0 and not first:
                        pe.wait_ge(b_vec.sem, b_vec.at(j - 1, "yd" if b else "yh"))

                products(pe, r, q, lambda c: br_hi[b][:, 2 * (q % 4) + c, :], lambda c: br_lo[b][:, 2 * (q % 4) + c, :],
                         4 * b, q % 4, 4, free, by_bank=False)

        def pool_branch(pool, j, first=False):
            if not first:
                pool.wait_ge(b_vec.sem, b_vec.at(j - 1, "yd"))
            for b, tile in enumerate((GHT, GDT)):
                pool.dma_start(gates[:, b], uT[tile:tile + 16].rearrange("c p t -> p c t")[
                    :, bass.ds(4 * j, 4), :]).then_inc(gates_landed, 16)

        def act_set_out(act, s, par):
            m_act.begin()
            act.wait_ge(granule_used, R_OUT + 8 * s + 8)
            m_act.done(act.activation(mixed[:, bass.ds(4 * s, 4), :], ps[:, 4 * par:4 * par + 4, 0:T], ACT.Copy), "copy")
            act.wait_ge(m_vec.sem, m_vec.at(s - 2, "part"))
            m_act.done(act.activation(stage[par][:, :, :], ps[:, 4 * par:4 * par + 4, 0:T], ACT.Square), "sq")

        def vec_squares(dve, buf, st, rnd, part, total):
            st.done(dve.tensor_reduce(sq_part[:, :], buf[:, :, :].rearrange("p m t -> p t m"), AX_X, ALU.add), part)
            dve.wait_ge(st.sem, st.at(rnd, part))
            st.done(dve.tensor_tensor(sq_sum[:, :], sq_sum[:, :], sq_part[:, :], ALU.add), total)
            dve.wait_ge(st.sem, st.at(rnd, total))

        def vec_set_out(dve, s, par):
            m_vec.begin()
            dve.wait_ge(m_act.sem, m_act.at(s, "sq"))
            vec_squares(dve, stage[par], m_vec, s, "part", "sum")

        def out_sets(do_granule, eng, after):
            with eng.Fori(0, BLOCKS // 2) as i:
                for par in range(2):
                    for q in range(8):
                        do_granule(2 * i + par, par, q, R_OUT + 16 * i + 8 * par + q, R_OUT // 8 + 2 * i + par + 1)
                        if par == 1 and q == 1 and after:
                            after(eng, 2 * i, 0)
                if after:
                    after(eng, 2 * i + 1, 1)

        HB = D_FF // 512

        def act_hidden(act, j, first=False):
            for q in range(16):
                split_hi(act, R_UP + 16 * j + q, q % 8, R_UP // 8 + 2 * j + q // 8 + 1)
                if first and q == 1:
                    e_act_root(act)
                if q == 10:
                    f_act.begin()
                    act.wait_ge(f_vec.sem, f_vec.at(j, "g"))
                    f_act.done(act.activation(stage[1][:, :, :], stage[0][:, :, :], ACT.Exp, scale=-1.0), "e")

        def e_act_root(act):
            act.wait_ge(e_pe2.sem, e_pe2.at(0, "ss"))
            e_act.done(act.activation(rs_ffn[:, :], ps[:, 7, 0:T], ACT.Sqrt, scale=1.0 / D_MODEL,
                                      bias=eps_c[:, 0:1]), "rt2")

        def times_root(dve, dst, bank):
            return dve.tensor_tensor(dst[:, :, :], ps[:, bank:bank + 4, 0:T],
                                     rs_ffn[:, :].unsqueeze(1).broadcast_to([P, 4, T]), ALU.mult)

        def vec_hidden(dve, j, first=False):
            def chain(ins, name):
                f_vec.done(ins, name)
                dve.wait_ge(f_vec.sem, f_vec.at(j, name))

            for q in range(16):
                split_lo(dve, R_UP + 16 * j + q, q % 8)
                if first and q == 1:
                    dve.wait_ge(e_act.sem, e_act.at(0, "rt2"))
                    e_vec.done(dve.reciprocal(rs_ffn[:, :], rs_ffn[:, :]), "rs2")
                    dve.wait_ge(e_vec.sem, e_vec.at(0, "rs2"))
                if not first and q == 1:
                    vec_up(dve, j - 1)
                if q == 9:
                    f_vec.begin()
                    dve.wait_ge(granule_used, R_UP + 16 * j + 8)
                    chain(times_root(dve, stage[0], 0), "g")
                if q == 11:
                    dve.wait_ge(f_act.sem, f_act.at(j, "e"))
                    chain(dve.tensor_scalar(stage[1][:, :, :], stage[1][:, :, :], 1.0, None, ALU.add), "one")
                    chain(dve.reciprocal(stage[1][:, :, :], stage[1][:, :, :]), "inv")
                    chain(dve.tensor_tensor(stage[0][:, :, :], stage[0][:, :, :], stage[1][:, :, :], ALU.mult), "gs")

        def vec_up(dve, j):
            dve.wait_ge(granule_used, R_UP + 16 * j + 16)
            f_vec.done(times_root(dve, stage[1], 4), "u")
            dve.wait_ge(f_vec.sem, f_vec.at(j, "u"))
            f_vec.done(dve.tensor_tensor(hidden[:, bass.ds(4 * j, 4), :], stage[0][:, :, :], stage[1][:, :, :],
                                         ALU.mult), "act")
            dve.wait_ge(f_vec.sem, f_vec.at(j, "act"))

        def pe_hidden(pe, j, first=False):
            for q in range(16):
                if first and q < 8 and q % 2 == 0:
                    pe.wait_ge(e_vec.sem, e_vec.at(0, f"l{q // 2}"))
                if first and q == 8:
                    pe.wait_ge(e_act.sem, e_act.at(0, "rt2"))

                def free(m):
                    if m == 0 and not first:
                        pe.wait_ge(f_vec.sem, f_vec.at(j - 1, "g" if q < 8 else "u"))

                products(pe, R_UP + 16 * j + q, q % 8, lambda c: h2_hi[:, 2 * (q % 8) + c, :],
                         lambda c: h2_lo[:, 2 * (q % 8) + c, :], 4 * (q // 8), q % 8, 8, free, by_bank=False)

        DOWN = FT_N

        def down(eng, do):
            for pas in range(2):
                def one(k, q, i):
                    at = R_DOWN + DOWN * pas + q
                    do(pas, k, at + 8 * i, at % 8, at // 8 + i + 1, q)
                for k in range(4):
                    one(k, k, 0)
                with eng.Fori(0, (DOWN - 4) // 8) as i:
                    for q in range(4, 12):
                        one(8 * i + q, q, i)

        def act_out(act, pas):
            g_act.begin()
            for m in range(8):
                if m < 7:
                    act.wait_ge(down_done, 7 * (5 * pas + 4) + m + 1)
                else:
                    act.wait_ge(granule_used, R_DOWN + DOWN * (pas + 1))
                g_act.done(act.activation(ffn[:, 8 * pas + m, :], ps[:, m, 0:T], ACT.Copy), f"c{m}")

        def act_out_sq(act, pas):
            act.wait_ge(g_act.sem, g_act.at(pas, "c7"))
            if pas:
                act.wait_ge(g_vec.sem, g_vec.at(0, "s1"))
            for b in range(2):
                k = 8 * pas + 4 * b
                g_act.done(act.activation(stage[b][:, :, :], ffn[:, k:k + 4, :], ACT.Square), f"q{b}")

        def vec_out_sq(dve, pas):
            g_vec.begin()
            for b in range(2):
                dve.wait_ge(g_act.sem, g_act.at(pas, f"q{b}"))
                vec_squares(dve, stage[b], g_vec, pas, f"p{b}", f"s{b}")

        def r_use(r):
            return r // RAW + 1

        def sync_rest(sp):
            sp.wait_ge(h_pool.sem, h_pool.last(HEADS - 1))
            sp.dma_start(pages[:, :], pt).then_inc(pages_landed, 16)
            rounds(sp, sync_mix)
            with sp.Fori(0, BLOCKS) as j:
                for q in range(8):
                    load(sp, R_BRANCH + 8 * j + q, q, branch_w(j, q))
            with sp.Fori(0, BLOCKS) as j:
                for q in range(8):
                    load(sp, R_OUT + 8 * j + q, q, w_granule(w_out, q, j))
            with sp.Fori(0, HB) as j:
                for q in range(16):
                    load(sp, R_UP + 16 * j + q, q % 8, w_granule(w_up, q % 8, j if q < 8 else j + HB))
            down(sp, lambda pas, k, r, slot, use, q: load(sp, r, slot, w_dn.rearrange("(k p) n -> k p n", p=P)[
                bass.ds(k, 1), :, 1024 * pas:1024 * pas + 1024].rearrange("a p n -> (a p) n")))
            for t4 in range(4):
                for j, (t0, n) in enumerate(NT):
                    sp.wait_ge(y_act.sem, y_act.at(0, f"o{3 * t4 + j}"))
                    cols = slice(512 * t4, 512 * t4 + 512)
                    sp.dma_start(y_p[t0:t0 + n, cols] if j < 2 else y_s[:, cols], y_tok[0:n, j, cols]).then_inc(y_stored, 16)
            sp.wait_ge(y_stored, 16 * 12)
            sp.wait_ge(u_stored, 16 * SETS_IN)

        def act_rest(act):
            act.sem_inc(k_act.sem, len(k_act.names))
            act.sem_inc(v_act.sem, len(v_act.names))
            act.wait_ge(q_zero, 1)
            rounds(act, act_mix)
            act.wait_ge(k_vec.sem, k_vec.at(NB - 1, "og"))
            act.wait_ge(v_used, PAGES * NB + 2)
            for b in range(2):
                ins = act.activation(br_hi[0][:, half[b], :], o_hg[:, half[b], :], ACT.Copy)
            d_act.done(ins, "hh")
            act.wait_ge(v_vec.sem, v_vec.at(NB - 1, "o"))
            for b in range(2):
                d_act.done(act.activation(stage[b][:, :, :], o_da[:, half[b], :], ACT.Square), f"sq{b}")
            act_branch(act, 0, first=True)
            with act.Fori(1, BLOCKS) as j:
                act_branch(act, j)
            act_merged(act, BLOCKS - 1)
            act.sem_inc(m_act.sem, 2 * len(m_act.names))
            out_sets(lambda s, par, q, r, use: split_hi(act, r, q, use), act, act_set_out)
            act.wait_ge(e_pe.sem, e_pe.at(0, "ss"))
            e_act.done(act.activation(rs_mix[:, :], ps[:, 0, 0:T], ACT.Sqrt, scale=1.0 / D_MODEL,
                                      bias=eps_c[:, 0:1]), "rt")
            for b in range(4):
                act.wait_ge(e_vec.sem, e_vec.at(0, f"x{b}"))
                for g in range(4 * b, 4 * b + 4):
                    ins = act.activation(h2_hi[:, g, :], o_all[:, g, :], ACT.Copy, scale=nrm_w[:, 2, g:g + 1])
                e_act.done(ins, f"h{b}")
                if b >= 2:
                    act.wait_ge(e_vec.sem, e_vec.at(0, f"p{b - 2}"))
                e_act.done(act.activation(stage[b % 2][:, :, :], o_all[:, 4 * b:4 * b + 4, :], ACT.Square), f"sq{b}")
            act_hidden(act, 0, first=True)
            with act.Fori(1, HB) as j:
                act_hidden(act, j)
            act.wait_ge(f_vec.sem, f_vec.at(HB - 1, "act"))
            act.wait_ge(granule_used, R_DOWN)

            def granule(pas, k, r, slot, use, q):
                act.wait_ge(raw_landed[slot], 16 * use)
                act.wait_ge(granule_used, r - HALVES + 1)
                act.activation(hid_hi[slot % HALVES][:, :], hidden[:, bass.ds(k, 1), :].rearrange("p a t -> p (a t)"), ACT.Copy)
                act.activation(w_hi[slot % HALVES][:, :], raw[slot][:, :], ACT.Copy).then_inc(hi_ready, 1)
                if pas and q == 1:
                    act_out(act, 0)
                if pas and q == 3:
                    act_out_sq(act, 0)

            down(act, granule)
            act_out(act, 1)
            act_out_sq(act, 1)
            act.wait_ge(y_pe.sem, y_pe.at(0, "ss"))
            y_act.done(act.activation(rs_mix[:, :], ps[:, 0, 0:T], ACT.Sqrt, scale=1.0 / D_MODEL,
                                      bias=eps_c[:, 0:1]), "rt")
            for k in range(12):
                t4, j = k // 3, k % 3
                n = NT[j][1]
                act.wait_ge(y_pe.sem, y_pe.at(0, f"t{k}"))
                y_act.done(act.activation(y_tok[0:n, j, 512 * t4:512 * t4 + 512], ps[0:n, k % 8, :], ACT.Copy), f"o{k}")

        def vec_rest(dve):
            dve.sem_inc(k_vec.sem, len(k_vec.names))
            dve.sem_inc(v_vec.sem, len(v_vec.names))
            dve.wait_ge(h_pe.sem, h_pe.last(HEADS - 1))
            dve.wait_ge(h_act.sem, h_act.last(HEADS - 1))
            dve.wait_ge(h_pool.sem, h_pool.last(HEADS - 1))
            dve.wait_ge(granule_used, R_MIX)
            dve.memset(q_hi[:, :, :].bitcast(F32), 0.0)
            dve.memset(q_lo[:, :, :].bitcast(F32), 0.0).then_inc(q_zero, 1)
            dve.wait_ge(q_zero, 1)
            rounds(dve, vec_mix)
            dve.wait_ge(d_act.sem, d_act.at(0, "hh"))
            for b in range(2):
                ins = dve.tensor_tensor(br_lo[0][:, half[b], :], o_hg[:, half[b], :],
                                        br_hi[0][:, half[b], :].bitcast(F32), ALU.subtract)
            d_vec.done(ins, "hl")
            vec_branch(dve, 0, first=True)
            with dve.Fori(1, BLOCKS) as j:
                vec_branch(dve, j)
            vec_merge(dve, BLOCKS - 1)
            vec_merged(dve, BLOCKS - 1)
            dve.sem_inc(m_vec.sem, 2 * len(m_vec.names))
            dve.memset(sq_sum[:, :], 0.0).then_inc(sums_zero, 1)
            dve.wait_ge(sums_zero, 1)
            out_sets(lambda s, par, q, r, use: split_lo(dve, r, q), dve, vec_set_out)

            def chain(ins, name, st=e_vec):
                st.done(ins, name)
                dve.wait_ge(st.sem, st.at(0, name))

            dve.wait_ge(e_act.sem, e_act.at(0, "rt"))
            dve.memset(sq_sum[:, :], 0.0).then_inc(sums_zero, 1)
            dve.wait_ge(sums_zero, 2)
            chain(dve.reciprocal(rs_mix[:, :], rs_mix[:, :]), "rs")
            dve.wait_ge(x_back, 16)
            for b in range(4):
                for g in range(4 * b, 4 * b + 4):
                    ins = dve.scalar_tensor_tensor(mixed[:, g, :], mixed[:, g, :], nrm_w[:, 1, g:g + 1],
                                                   rs_mix[:, :], ALU.mult, ALU.mult)
                four = slice(4 * b, 4 * b + 4)
                chain(ins, f"n{b}")
                chain(dve.tensor_tensor(o_all[:, four, :], o_all[:, four, :], mixed[:, four, :], ALU.add), f"x{b}")
                dve.wait_ge(e_act.sem, e_act.at(0, f"h{b}"))
                for g in range(4 * b, 4 * b + 4):
                    ins = dve.scalar_tensor_tensor(h2_lo[:, g, :], o_all[:, g, :], nrm_w[:, 2, g:g + 1],
                                                   h2_hi[:, g, :].bitcast(F32), ALU.mult, ALU.subtract)
                e_vec.done(ins, f"l{b}")
                dve.wait_ge(e_act.sem, e_act.at(0, f"sq{b}"))
                vec_squares(dve, stage[b % 2], e_vec, 0, f"p{b}", f"s{b}")
            vec_hidden(dve, 0, first=True)
            with dve.Fori(1, HB) as j:
                vec_hidden(dve, j)
            vec_up(dve, HB - 1)
            dve.memset(sq_sum[:, :], 0.0).then_inc(sums_zero, 1)
            dve.wait_ge(sums_zero, 3)

            def granule(pas, k, r, slot, use, q):
                dve.wait_ge(hi_ready, r + 1)
                dve.tensor_tensor(hid_lo[slot % HALVES][:, :], hidden[:, bass.ds(k, 1), :].rearrange("p a t -> p (a t)"),
                                  hid_hi[slot % HALVES][:, :].bitcast(F32), ALU.subtract)
                dve.tensor_tensor(w_lo[slot % HALVES][:, :], raw[slot][:, :],
                                  w_hi[slot % HALVES][:, :].bitcast(F32), ALU.subtract).then_inc(lo_ready, 1)
                if pas and q == 3:
                    vec_out_sq(dve, 0)

            down(dve, granule)
            vec_out_sq(dve, 1)
            dve.wait_ge(y_act.sem, y_act.at(0, "rt"))
            chain(dve.reciprocal(rs_mix[:, :], rs_mix[:, :]), "rs", y_vec)
            for b in range(4):
                for g in range(4 * b, 4 * b + 4):
                    ins = dve.scalar_tensor_tensor(ffn[:, g, :], ffn[:, g, :], nrm_w[:, 3, g:g + 1],
                                                   rs_mix[:, :], ALU.mult, ALU.mult)
                four = slice(4 * b, 4 * b + 4)
                chain(ins, f"n{b}", y_vec)
                chain(dve.tensor_tensor(ffn[:, four, :], o_all[:, four, :], ffn[:, four, :], ALU.add), f"y{b}", y_vec)

        def pe_rest(pe):
            pe.sem_inc(k_pe.sem, len(k_pe.names))
            pe.sem_inc(v_pe.sem, len(v_pe.names))
            pe.sem_inc(v_used, 2)
            pe.wait_ge(set_out, 4 * SETS_IN)
            pe.wait_ge(h_act.sem, h_act.last(HEADS - 1))
            pe.wait_ge(h_vec.sem, h_vec.last(HEADS - 1))
            rounds(pe, pe_mix)
            pe.wait_ge(v_used, PAGES * NB + 2)
            pe.sem_inc(granule_used, R_BRANCH - R_MIX)
            pe_branch(pe, 0, first=True)
            with pe.Fori(1, BLOCKS) as j:
                pe_branch(pe, j)
            pe.wait_ge(b_vec.sem, b_vec.last(BLOCKS - 1))

            def granule(s, par, q, r, use):
                def free(m):
                    if m == 0:
                        pe.wait_ge(m_act.sem, m_act.at(s - 2, "sq"))
                products(pe, r, q, lambda c: m_hi[:, 2 * q + c, :], lambda c: m_lo[:, 2 * q + c, :],
                         4 * par, q, 8, free, by_bank=False)

            out_sets(granule, pe, None)
            pe.wait_ge(m_vec.sem, m_vec.last(BLOCKS - 1))
            e_pe.done(pe.matmul(ps[:, 0, 0:T], ones[:, :], sq_sum[:, :], start=True, stop=True), "ss")
            pe.wait_ge(e_act.sem, e_act.at(0, "rt"))
            pe.wait_ge(e_vec.sem, e_vec.at(0, "s3"))
            e_pe2.done(pe.matmul(ps[:, 7, 0:T], ones[:, :], sq_sum[:, :], start=True, stop=True), "ss")
            pe_hidden(pe, 0, first=True)
            with pe.Fori(1, HB) as j:
                pe_hidden(pe, j)
            pe.wait_ge(f_vec.sem, f_vec.at(HB - 1, "u"))

            def down_granule(pas, k, r, slot, use, q):
                pe.wait_ge(lo_ready, r + 1)
                wh, wl = w_hi[slot % HALVES], w_lo[slot % HALVES]
                xh, xl = hid_hi[slot % HALVES][:, :], hid_lo[slot % HALVES][:, :]
                for m in range(8):
                    if pas and q == 0:
                        pe.wait_ge(g_act.sem, g_act.at(0, f"c{m}"))
                    c = slice(P * m, P * m + P)
                    add = dict(start=False, stop=q > 3, skip_group_check=q > 3)
                    pe.matmul(ps[:, m, 0:T], wh[:, c], xh, **dict(add, start=q == 0))
                    pe.matmul(ps[:, m, 0:T], wl[:, c], xh, **add)
                    ins = pe.matmul(ps[:, m, 0:T], wh[:, c], xl, **dict(add, stop=q >= 3))
                    if q == 11 and m < 7:
                        ins.then_inc(down_done, 1)
                ins.then_inc(granule_used, 1)

            down(pe, down_granule)
            pe.wait_ge(g_vec.sem, g_vec.at(1, "s1"))
            y_pe.done(pe.matmul(ps[:, 0, 0:T], ones[:, :], sq_sum[:, :], start=True, stop=True), "ss")
            pe.wait_ge(y_act.sem, y_act.at(0, "rt"))
            for k in range(12):
                t4, j = k // 3, k % 3
                t0, n = NT[j]
                if j == 0:
                    pe.wait_ge(y_vec.sem, y_vec.at(0, f"y{t4}"))
                if k >= 8:
                    pe.wait_ge(y_act.sem, y_act.at(0, f"o{k - 8}"))
                for c in range(4):
                    ins = pe.transpose(ps[0:n, k % 8, P * c:P * c + P], ffn[:, 4 * t4 + c, t0:t0 + n], ident[:, :])
                y_pe.done(ins, f"t{k}")

        def pool_rest(pool):
            pool.wait_ge(h_pe.sem, h_pe.last(HEADS - 1))
            pool.wait_ge(h_vec.sem, h_vec.last(HEADS - 1))
            pool.wait_ge(granule_used, R_MIX)
            pool.dma_start(q_all[:, :, :], uT[DQT:DQT + 8].rearrange("c p t -> p c t")[:, :, SEQ:T]).then_inc(mix_landed, 16)
            rows = [[P * BIAS_L, MAPS]]
            pool.dma_start(near[:, :], bass.AP(bias_rows.tensor, P - 1, rows + [[BIAS_L - 1, NQ], [1, NEAR]])).then_inc(mix_landed, 16)
            pool.dma_start(far[:, :], bass.AP(bias_rows.tensor, 0, rows + [[BIAS_L, NQ], [1, 2]])).then_inc(mix_landed, 16)
            rounds(pool, pool_mix)
            pool.wait_ge(v_used, PAGES * NB + 2)
            pool.wait_ge(v_pe.sem, v_pe.last(NB - 1))
            pool.wait_ge(v_vec.sem, v_vec.last(NB - 1))
            pool_branch(pool, 0, first=True)
            with pool.Fori(1, BLOCKS) as j:
                pool_branch(pool, j)
            pool.wait_ge(d_vec.sem, d_vec.at(0, "dl"))
            pool.dma_start(o_all[:, :, :], xT_keep.rearrange("c p t -> p c t")).then_inc(x_back, 16)


        @block.sync
        def _(sp):
            for j, (t0, n) in enumerate(NT):
                sp.dma_start(x_tok[j][0:n, :], xp[t0:t0 + n, :] if j < 2 else xs).then_inc(x_landed[j], 16)
            for dst, src in ((ident[:], c_ident), (nrm_w[:], nrm), (hg_w[:], hgw), (coef[:], c_coef),
                             (lb_t[:, 0:2, :], lbl), (lam_in[:], lamv.broadcast_to([P, 4, DH])),
                             (hot[:], c_hot), (tab[0:32, :], table), (scan_keep[:], c_scan),
                             (causal[:], c_causal), (own[:], c_own)):
                sp.dma_start(dst, src).then_inc(const_landed, 16)
            for r in range(RAW):
                load(sp, r, r, w_granule(w_in, r, 0), first=True)
            with sp.Fori(1, SETS_HEAD) as n:
                for q in range(8):
                    load(sp, 8 * n + q, q, w_granule(w_in, q, n))
            with sp.Fori(0, HEADS // 2) as i:
                for par in range(2):
                    h = 2 * i + par
                    n = SETS_HEAD + h
                    for q in range(8):
                        load(sp, 8 * n + q, q, w_granule(w_in, q, n))
                        if q == 4:
                            head_loads(sp, h, par)
            sync_rest(sp)

        @block.scalar
        def _(act):
            act.sem_inc(h_act.sem, 2 * len(h_act.names))
            act.wait_ge(u_pool.sem, u_pool.at(0, "zero"))
            for j, (t0, n) in enumerate(NT):
                act.wait_ge(x_landed[j], 16)
                if j:
                    act.wait_ge(u_act.sem, u_act.at(0, f"sq{j - 1}"))
                u_act.done(act.activation(x_sq[0:n, :], x_tok[j][0:n, :], ACT.Square,
                                          accum_out=x_rs[0:n, 0, j:j + 1]), f"sq{j}")
            act.wait_ge(u_pool.sem, u_pool.at(0, "mean"))
            u_act.done(act.activation(x_rs[:, 2, :], x_rs[:, 1, :], ACT.Sqrt), "root")
            act.wait_ge(u_vec.sem, u_vec.at(0, "lb_d"))
            u_act.done(act.activation(lb_t[:, 3:5, :], lb_t[:, 3:5, :], ACT.Exp), "lb_e")
            act.wait_ge(u_vec.sem, u_vec.at(0, "lam_d"))
            u_act.done(act.activation(lam_s[:, 2:4], lam_s[:, 0:2], ACT.Exp), "lam_e")
            for r in range(2):
                split_hi(act, r, r, 1, first=True)
            for g in tiles:
                act.wait_ge(u_pe.sem, u_pe.at(0, f"x{g}"))
                if g >= 8 and g % 4 == 0:
                    act.wait_ge(x_kept[g // 4 % 2], 16)
                u_act.done(act.activation(xT4[g // 4 % 2][:, g % 4, :], ps[:, g % 4, 0:T], ACT.Copy), f"x{g}")
                act.wait_ge(u_vec.sem, u_vec.at(0, f"h{g}"))
                u_act.done(act.activation(x_hi[:, g, :], hT[g % 2][:, :], ACT.Copy), f"h{g}")
                if g % 4 == 3:
                    act.wait_ge(u_act.sem, u_act.at(0, f"x{g}"))
                    act.dma_start(xT_keep[g - 3:g + 1].rearrange("c p t -> p c t"),
                                  xT4[g // 4 % 2][:, :, :]).then_inc(x_kept[g // 4 % 2], 16)
            for r in range(2, 8):
                split_hi(act, r, r, 1, first=r < HALVES)
            act_block(act, 1, 1)
            with act.Fori(1, SETS_HEAD // 2) as i:
                for par in range(2):
                    act_block(act, 2 * i + par, par)
            with act.Fori(0, HEADS // 2) as i:
                for par in range(2):
                    act_block(act, SETS_HEAD + 2 * i + par, par, (2 * i + par, i))
            read_set(act, SETS_IN - 1, R_MIX, 1)
            act_rest(act)

        @block.vector
        def _(dve):
            def chain(ins, name):
                u_vec.done(ins, name)
                dve.wait_ge(u_vec.sem, u_vec.at(0, name))

            dve.sem_inc(h_vec.sem, 2 * len(h_vec.names))
            dve.memset(eps_c[:, :], EPS)
            u_vec.done(dve.memset(ones[:, :], 1.0), "ones")
            dve.wait_ge(const_landed, CONSTS)
            u_vec.done(dve.memset(tab[32:33, :], -1e30), "tab")
            chain(dve.tensor_tensor(lb_t[:, 2, :], lb_t[:, 0, :], lb_t[:, 1, :], ALU.max), "lb_max")
            dve.tensor_tensor(lb_t[:, 3, :], lb_t[:, 0, :], lb_t[:, 2, :], ALU.subtract)
            u_vec.done(dve.tensor_tensor(lb_t[:, 4, :], lb_t[:, 1, :], lb_t[:, 2, :], ALU.subtract), "lb_d")
            lam4 = lam_in[:, :, :].rearrange("p (a b) d -> p b a d", b=2)
            chain(dve.tensor_tensor(lam_p[:, :, :], lam4[:, 0], lam4[:, 1], ALU.mult), "lam_p")
            u_vec.done(dve.tensor_reduce(lam_s[:, 0:2], lam_p[:, :, :], AX_X, ALU.add), "lam_d")
            dve.wait_ge(u_act.sem, u_act.at(0, "root"))
            chain(dve.reciprocal(x_rs[:, 2, :], x_rs[:, 2, :]), "rs_inv")
            for j in range(3):
                ins = dve.tensor_scalar(x_rsb[:, j, :], ones[:, :], x_rs[:, 2, j:j + 1], None, ALU.mult)
            u_vec.done(ins, "rsb")
            dve.wait_ge(u_pe.sem, u_pe.at(0, "bias"))
            u_vec.done(dve.tensor_copy(bias_vec[:, :], ps[0:MAPS, 6, 0:BIAS_L]), "bias_vec")
            dve.wait_ge(u_pe.sem, u_pe.at(0, "rs"))
            chain(dve.tensor_copy(rs_all[:, :], ps[:, 7, 0:T]), "rs")
            for g in tiles:
                dve.wait_ge(u_act.sem, u_act.at(0, f"x{g}"))
                if g >= 2:
                    dve.wait_ge(u_vec.sem, u_vec.at(0, f"l{g - 2}"))
                chain(dve.scalar_tensor_tensor(hT[g % 2][:, :], ps[:, g % 4, 0:T], nrm_w[:, 0, g:g + 1],
                                               rs_all[:, :], ALU.mult, ALU.mult), f"h{g}")
                dve.wait_ge(u_act.sem, u_act.at(0, f"h{g}"))
                u_vec.done(dve.tensor_tensor(x_lo[:, g, :], hT[g % 2][:, :],
                                             x_hi[:, g, :].bitcast(F32), ALU.subtract), f"l{g}")
                if g == 1:
                    for r in range(2):
                        split_lo(dve, r, r)
            for r in range(2, 8):
                split_lo(dve, r, r)
            chain(dve.tensor_tensor(lb_t[:, 5, :], lb_t[:, 3, :], lb_t[:, 4, :], ALU.add), "lb_s")
            chain(dve.reciprocal(lb_t[:, 5, :], lb_t[:, 5, :]), "lb_r")
            chain(dve.tensor_tensor(lb, lb_t[:, 3, :], lb_t[:, 5, :], ALU.mult), "lb")
            u_vec.done(dve.tensor_scalar(omlb, lb, -1.0, 1.0, ALU.mult, ALU.add), "omlb")
            u_vec.done(dve.memset(aT[:, :, :], 0.0), "aT")
            chain(dve.tensor_tensor(lam_s[:, 4:5], lam_s[:, 2:3], lam_s[:, 3:4], ALU.subtract), "lam1")
            chain(dve.tensor_scalar(lam_s[:, 5:6], lam_s[:, 4:5], LAM_INIT, None, ALU.add), "lam2")
            u_vec.done(dve.tensor_scalar(neg_lam[:, :], lam_s[:, 5:6], -1.0, None, ALU.mult), "neg")
            chain(dve.scalar_tensor_tensor(cf[:, :], lam_s[:, 5:6], coef[:, 1:2], coef[:, 0:1],
                                           ALU.mult, ALU.add), "cf")
            with dve.Fori(1, SETS_HEAD) as n:
                for q in range(8):
                    split_lo(dve, 8 * n + q, q)
            with dve.Fori(0, HEADS // 2) as i:
                for par in range(2):
                    h = 2 * i + par
                    for q in range(8):
                        split_lo(dve, R_HEAD + 8 * h + q, q)
                        vec_head(dve, q, par, h, i)
            vec_rest(dve)

        @block.tensor
        def _(pe):
            pe.sem_inc(h_pe.sem, 2 * len(h_pe.names))
            pe.wait_ge(const_landed, CONSTS)
            pe.wait_ge(u_vec.sem, u_vec.at(0, "tab"))
            u_pe.done(pe.matmul(ps[0:MAPS, 6, 0:BIAS_L], tab[:, :], hot[:, :], start=True, stop=True), "bias")

            def turn(g):
                if g >= 4:
                    pe.wait_ge(u_act.sem, u_act.at(0, f"x{g - 4}"))
                    pe.wait_ge(u_vec.sem, u_vec.at(0, f"h{g - 4}"))
                for j, (t0, n) in enumerate(NT):
                    ins = pe.transpose(ps[:, g % 4, t0:t0 + n], x_tok[j][0:n, g * P:(g + 1) * P],
                                       ident[0:n, 0:n])
                u_pe.done(ins, f"x{g}")

            for j in range(3):
                pe.wait_ge(x_landed[j], 16)
            pe.wait_ge(u_vec.sem, u_vec.at(0, "rsb"))
            for j, (t0, n) in enumerate(NT):
                ins = pe.matmul(ps[:, 7, t0:t0 + n], x_rsb[0:n, j, :], ident[0:n, 0:n], start=True, stop=True)
            u_pe.done(ins, "rs")
            for g in tiles:
                turn(g)
            pe.wait_ge(u_act.sem, u_act.last(0))
            pe.wait_ge(u_vec.sem, u_vec.at(0, f"l{KT - 1}"))

            def in_products(r, q, free):
                products(pe, r, q, lambda c: x_hi[:, 2 * q + c, :], lambda c: x_lo[:, 2 * q + c, :],
                         0, q, 8, free)

            for q in range(8):
                in_products(q, q, lambda m: None)
            with pe.Fori(1, SETS_HEAD) as n:
                for q in range(8):
                    in_products(8 * n + q, q, lambda m: pe.wait_ge(set_out, 4 * n + m - 3))
            with pe.Fori(0, HEADS // 2) as i:
                for par in range(2):
                    h = 2 * i + par
                    n = SETS_HEAD + h
                    for q in range(8):
                        in_products(8 * n + q, q, lambda m: pe.wait_ge(set_out, 4 * n + m - 3))
                        pe_head(pe, q, par, h, i)
            pe_rest(pe)

        @block.gpsimd
        def _(pool):
            pool.sem_inc(h_pool.sem, 2)
            pool.sem_inc(stage_free, 2)
            u_pool.done(pool.memset(x_rs[:, :, :], 1.0), "zero")
            pool.wait_ge(u_act.sem, u_act.at(0, "sq2"))
            u_pool.done(pool.tensor_scalar(x_rs[:, 1, :], x_rs[:, 0, :], 1.0 / D_MODEL, EPS, ALU.mult, ALU.add), "mean")
            pool.wait_ge(u_vec.sem, u_vec.at(0, "bias_vec"))
            pool.dma_start(bias_rows, bias_vec[:, :].unsqueeze(1).broadcast_to([MAPS, P, BIAS_L])).then_inc(bias_stored, 16)
            store_set(pool, 0, 0)
            with pool.Fori(0, (SETS_HEAD - 2) // 2) as i:
                for par in range(2):
                    store_set(pool, 2 * i + 1 + par, 1 - par)
            with pool.Fori(0, HEADS // 2) as i:
                for par in range(2):
                    h = 2 * i + par
                    store_set(pool, SETS_HEAD - 1 + h, 1 - par)
                    pool_head(pool, par, h)
            store_set(pool, SETS_IN - 1, 1)
            pool_rest(pool)


def bucket(dist):
    import math

    import numpy as np
    near = 16
    n = np.float32(max(dist, 1))
    far = near + int(np.log(n / np.float32(near)) / np.float32(math.log(128 / near)) * np.float32(near))
    return dist if dist < near else min(far, 31)


def kernel(**inputs):
    import numpy as np

    import concourse.bacc as bacc
    from concourse.bass_utils import run_bass_kernel_spmd

    a = {k: np.asarray(v) for k, v in inputs.items()}

    def cols(v):
        return v.reshape(-1, P).T

    scan = np.ones((P, T), np.float32)
    scan[:, 0:SEQ:CHUNK] = 0
    scan[:, SEQ::NQ] = 0
    i = np.arange(CHUNK)
    tri = (i[:, None] <= i[None, :]).astype(np.int32)
    same = (i[:, None] // NQ == i[None, :] // NQ).astype(np.int32)
    hot = np.zeros((33, BIAS_L), np.float32)
    for j in range(BIAS_L):
        dist = 255 - j
        hot[32 if dist < 0 else bucket(dist), j] = 1
    coef = np.zeros((P, 2), np.float32)
    coef[:CHUNK, 0], coef[CHUNK:, 1] = 1, -1
    arrays = {
        "xp": a["x_prompt"][0], "xs": a["x_sample"].reshape(NB * NQ, D_MODEL),
        "ck": a["cache_k"][0].reshape(POOL, PAGE, MAPS * DH), "cv": a["cache_v"][0].reshape(POOL, PAGE, HEADS * DV),
        "st": a["state_hgrn"][0], "pt": a["page_table"].astype(np.int32),
        "w_in": a["w_in"][0], "w_hg": a["w_branch_hg"][0], "w_da": a["w_branch_da"][0], "w_out": a["w_out"][0],
        "w_up": a["w_ffn_up"][0], "w_dn": a["w_ffn_down"][0],
        "nrm": np.stack([cols(a[k][0]) for k in ("norm_mix_pre", "norm_mix_post", "norm_ffn_pre", "norm_ffn_post")], 1),
        "hgw": np.stack([a["hg_norm_w"][0], a["da_subln_w"][0]], 1),
        "lbl": np.stack([cols(v) for v in a["hg_lb_logits"]], 1),
        "lamv": np.stack([a[f"da_lambda_{k}"][0] for k in ("q1", "k1", "q2", "k2")])[None],
        "table": a["rel_bias_table"],
        "c_ident": np.eye(P, dtype=np.float32), "c_scan": scan,
        "c_causal": np.stack([tri] * 4 + [tri * same], 1),
        "c_own": (i[:, None] // NQ == np.arange(NB)[None, :]).astype(np.float32),
        "c_hot": hot, "c_coef": coef,
    }
    outs = {"y_p": (SEQ, D_MODEL), "y_s": (NB * NQ, D_MODEL), "k_p": (SEQ, MAPS, DH), "v_p": (SEQ, HEADS, DV),
            "h_p": (HEADS, P, DV), "k_s": (NB * NQ, MAPS, DH), "v_s": (NB * NQ, HEADS, DV),
            "h_s": (NB, HEADS, P, DV)}
    nc = bacc.Bacc("TRN2", target_bir_lowering=False, num_devices=1)
    arrays = {k: np.ascontiguousarray(v) for k, v in arrays.items()}
    args = [nc.dram_tensor(k, v.shape, mybir.dt.from_np(v.dtype), kind="ExternalInput").ap() for k, v in arrays.items()]
    args += [nc.dram_tensor(k, s, F32, kind="ExternalOutput").ap() for k, s in outs.items()]
    build(nc, *args)
    r = run_bass_kernel_spmd(nc, [arrays], core_ids=[0]).results[0]
    return (r["y_p"].reshape(1, SEQ, D_MODEL), r["y_s"].reshape(NB, NQ, D_MODEL),
            r["k_p"].reshape(1, 1, SEQ, MAPS, DH), r["v_p"].reshape(1, 1, SEQ, HEADS, DV),
            r["h_p"].reshape(1, 1, HEADS, P, DV), r["k_s"].reshape(1, NB, NQ, MAPS, DH),
            r["v_s"].reshape(1, NB, NQ, HEADS, DV), r["h_s"].reshape(1, NB, HEADS, P, DV))
```

```python
from contextlib import ExitStack

import concourse.bass as bass
from concourse import mybir

ALU = mybir.AluOpType
ACT = mybir.ActivationFunctionType
AX_X = mybir.AxisListType.X
F32 = mybir.dt.float32
F32R = mybir.dt.float32r
I32 = mybir.dt.int32

P = 128
D_MODEL, D_FF = 2048, 5632
SEQ, NB, NQ = 256, 8, 8
T = SEQ + NB * NQ
HEADS, MAPS, DH, DV = 8, 16, 64, 128
PAGE, PAGES, POOL = 128, 16, 160
PAST = PAGE * PAGES
CHUNK, CHUNKS = 64, T // 64
N_IN = 88
QT, FT, IT, OT, DQT, DKT, DVT, GHT, GDT = 0, 8, 16, 24, 32, 40, 48, 56, 72
EPS = 1e-6
LAM_INIT = 0.2
SCALE = DH ** -0.5
KT = D_MODEL // P
FT_N = D_FF // P
RAW, HALVES = 8, 4
BIAS_L = 384
NEAR = P + NQ

SETS_IN, SETS_HEAD = 22, 14
R_IN = 0
R_HEAD = R_IN + 8 * SETS_HEAD
R_MIX = R_IN + 8 * SETS_IN
R_BRANCH = R_MIX + 2 * PAGES * NB
R_OUT = R_BRANCH + 32
R_UP = R_OUT + 32
R_DOWN = R_UP + 16 * (D_FF // 512)


class Steps:

    def __init__(self, sem, names, lead=0):
        self.sem, self.names, self.lead, self.next = sem, names.split(), lead, 0

    def at(self, rnd, name):
        return len(self.names) * (rnd + self.lead) + self.names.index(name) + 1

    def begin(self):
        self.next = 0

    def done(self, ins, name):
        assert self.names[self.next] == name, (self.names[self.next], name)
        self.next += 1
        ins.then_inc(self.sem, 1)

    def last(self, rnd):
        return self.at(rnd, self.names[-1])


def build(nc, xp, xs, ck, cv, st, pt, w_in, w_hg, w_da, w_out, w_up, w_dn, nrm, hgw, lbl, lamv,
          table, c_ident, c_scan, c_causal, c_own, c_hot, c_coef,
          y_p, y_s, k_p, v_p, h_p, k_s, v_s, h_s):
    with ExitStack() as ctx:
        def sb(name, shape, dt=F32, where=None):
            return (where or ctx).enter_context(nc.sbuf_tensor(name, shape, dt))

        def sem(name):
            return ctx.enter_context(nc.semaphore(name))

        uT = nc.dram_tensor("uT", (N_IN, P, T), F32, kind="Internal").ap()
        bias_rows = nc.dram_tensor("bias_rows", (MAPS, P, BIAS_L), F32, kind="Internal").ap()
        new_scores = nc.dram_tensor("new_scores", (MAPS, NB * NQ, NB * NQ), F32, kind="Internal").ap()
        xT_keep = nc.dram_tensor("xT_keep", (KT, P, T), F32, kind="Internal").ap()

        raw = [sb(f"raw{j}", [P, 1024]) for j in range(RAW)]
        w_hi = [sb(f"w_hi{j}", [P, 1024], F32R) for j in range(HALVES)]
        w_lo = [sb(f"w_lo{j}", [P, 1024], F32R) for j in range(HALVES)]
        ident = sb("ident", [P, P])
        ones = sb("ones", [P, P])
        nrm_w = sb("nrm_w", [P, 4, KT])
        hg_w = sb("hg_w", [P, 2])
        eps_c = sb("eps_c", [P, 1])
        coef = sb("coef", [P, 2])
        cf = sb("cf", [P, 1])
        neg_lam = sb("neg_lam", [P, 1])
        lam_s = sb("lam_s", [P, 8])
        pages = sb("pages", [1, NB * PAGES], I32)
        o_all = sb("o_all", [P, KT, T])
        o_hg, o_da = o_all[:, 0:HEADS, :], o_all[:, HEADS:, :]
        stage = [sb(f"stage{j}", [P, 4, T]) for j in range(2)]
        ps = ctx.enter_context(nc.psum_tensor("ps", [P, 8, 512], F32))

        at_in = ExitStack()
        x_hi = sb("x_hi", [P, KT, T], F32R, at_in)
        x_lo = sb("x_lo", [P, KT, T], F32R, at_in)
        scan_keep = sb("scan_keep", [P, T], F32, at_in)
        causal = sb("causal", [CHUNK, CHUNKS, CHUNK], I32, at_in)
        own = sb("own", [CHUNK, NB], F32, at_in)
        lb_t = sb("lb_t", [P, 8, HEADS], F32, at_in)
        lb, omlb = lb_t[:, 6, :], lb_t[:, 7, :]
        aT = sb("aT", [CHUNK, CHUNKS, CHUNK], F32, at_in)
        at_x = ExitStack()
        x_tok = [sb(f"x_tok{j}", [P, D_MODEL], F32, at_x) for j in range(3)]
        x_sq = sb("x_sq", [P, D_MODEL], F32, at_x)
        xT4 = [sb(f"xT4_{j}", [P, 4, T], F32, at_x) for j in range(2)]
        hT = [sb(f"hT{j}", [P, T], F32, at_x) for j in range(2)]
        x_rs = sb("x_rs", [P, 3, 3], F32, at_x)
        x_rsb = sb("x_rsb", [P, 3, P], F32, at_x)
        rs_all = sb("rs_all", [P, T], F32, at_x)
        lam_in = sb("lam_in", [P, 4, DH], F32, at_x)
        lam_p = sb("lam_p", [P, 2, DH], F32, at_x)
        hot = sb("hot", [33, BIAS_L], F32, at_x)
        tab = sb("tab", [33, MAPS], F32, at_x)
        bias_vec = sb("bias_vec", [MAPS, BIAS_L], F32, at_x)
        at_x.close()
        at_h = ExitStack()
        hin = [sb(f"hin{j}", [P, 3, T], F32, at_h) for j in range(2)]
        mq = [sb(f"mq{j}", [P, T], F32, at_h) for j in range(2)]
        mk = [sb(f"mk{j}", [P, T], F32, at_h) for j in range(2)]
        mv = [sb(f"mv{j}", [P, T], F32, at_h) for j in range(2)]
        s0 = [sb(f"s0{j}", [P, NB, DV], F32, at_h) for j in range(2)]
        mb = [sb(f"mb{j}", [P, 2, 2 * P], F32, at_h) for j in range(2)]
        kin = sb("kin", [P, T], F32, at_h)
        fg = sb("fg", [P, T], F32, at_h)
        lg = sb("lg", [P, T], F32, at_h)
        G = sb("G", [P, T], F32, at_h)
        eG = sb("eG", [P, T], F32, at_h)
        kg = sb("kg", [P, T], F32, at_h)
        kd = sb("kd", [P, T], F32, at_h)
        qg = sb("qg", [P, T], F32, at_h)
        k_tok = sb("k_tok", [P, 3, P], F32, at_h)
        v_tok = sb("v_tok", [P, 3, P], F32, at_h)
        i_tok = sb("i_tok", [CHUNK, CHUNKS, DV], F32, at_h)
        kd_tok = sb("kd_tok", [CHUNK, CHUNKS, P], F32, at_h)
        i_own = sb("i_own", [CHUNK, NB, DV], F32, at_h)
        state = sb("state", [P, 4, DV], F32, at_h)
        s_new = sb("s_new", [P, NB, DV], F32, at_h)
        s_at = sb("s_at", [P, 2, 3 * P], F32, at_h)
        s_sm = sb("s_sm", [CHUNK, 2, CHUNK], F32, at_h)
        mx = sb("mx", [P, 4], F32, at_h)
        nmx = sb("nmx", [P, 4], F32, at_h)
        sm = sb("sm", [P, 4], F32, at_h)
        rc = sb("rc", [P, 4], F32, at_h)
        pd2 = sb("pd2", [P, 3 * P], F32, at_h)
        pd = sb("pd", [P, 3 * P], F32, at_h)
        pdt = sb("pdt", [P, 3, P], F32, at_h)
        at_h.close()
        at_in.close()

        at_mix = ExitStack()
        kt_hi = [sb(f"kt_hi{j}", [P, 8, 4 * PAGE], F32R, at_mix) for j in range(2)]
        kt_lo = [sb(f"kt_lo{j}", [P, 8, 4 * PAGE], F32R, at_mix) for j in range(2)]
        q_hi = sb("q_hi", [P, 8, P], F32R, at_mix)
        q_lo = sb("q_lo", [P, 8, P], F32R, at_mix)
        p_hi = sb("p_hi", [P, PAGES, P], F32R, at_mix)
        p_lo = sb("p_lo", [P, PAGES, P], F32R, at_mix)
        p_new = sb("p_new", [NQ, P], F32, at_mix)
        v_new = sb("v_new", [NQ, HEADS * DV], F32, at_mix)
        s_all = sb("s_all", [P, PAST + NQ], F32, at_mix)
        o_rows = sb("o_rows", [P, HEADS * DV], F32, at_mix)
        o_second = sb("o_second", [P, HEADS, NQ], F32, at_mix)
        q_all = sb("q_all", [P, 8, NB * NQ], F32, at_mix)
        near = sb("near", [P, NEAR], F32, at_mix)
        s_n = sb("s_n", [P, NQ], F32, at_mix)
        far = sb("far", [P, 2], F32, at_mix)
        mxk = sb("mxk", [P, 6], F32, at_mix)
        l_all = sb("l_all", [P, 2], F32, at_mix)
        w_row = sb("w_row", [P, 1], F32, at_mix)
        at_mix.close()

        at_branch = ExitStack()
        sb("below_branch", [P, 4, T], F32, at_branch)
        br_hi = [sb(f"br_hi{b}", [P, HEADS, T], F32R, at_branch) for b in range(2)]
        br_lo = [sb(f"br_lo{b}", [P, HEADS, T], F32R, at_branch) for b in range(2)]
        m_hi = sb("m_hi", [P, KT, T], F32R, at_branch)
        m_lo = sb("m_lo", [P, KT, T], F32R, at_branch)
        gates = sb("gates", [P, 2, 4, T], F32, at_branch)
        at_branch.close()
        at_end = ExitStack()
        sb("below_end", [P, 4, T], F32, at_end)
        ffn = sb("ffn", [P, KT, T], F32, at_end)
        sb("below_y_tok", [P, 16, T], F32, at_end)
        y_tok = sb("y_tok", [P, 3, D_MODEL], F32, at_end)
        at_end.close()
        sq_sum, sq_part, rs_mix, rs_ffn = (sb(n, [P, T]) for n in ("sq_sum", "sq_part", "rs_mix", "rs_ffn"))
        h2_hi = sb("h2_hi", [P, KT, T], F32R)
        h2_lo = sb("h2_lo", [P, KT, T], F32R)
        at_out = ExitStack()
        sb("below_mixed", [P, 2 * KT, T], F32, at_out)
        mixed = sb("mixed", [P, KT, T], F32, at_out)
        at_out.close()
        hidden = sb("hidden", [P, FT_N, T])
        hid_hi = [sb(f"hid_hi{j}", [P, T], F32R) for j in range(HALVES)]
        hid_lo = [sb(f"hid_lo{j}", [P, T], F32R) for j in range(HALVES)]
        n_sq, n_gate, n_rs, n_e = (stage[0][:, m, :] for m in range(4))
        n_sq2, n_rs2 = (stage[1][:, m, 0:SEQ] for m in range(2))

        raw_landed = [sem(f"raw_landed{j}") for j in range(RAW)]
        hi_ready = sem("hi_ready")
        lo_ready = sem("lo_ready")
        granule_used = sem("granule_used")
        set_done = sem("set_done")
        set_out = sem("set_out")
        stage_free = sem("stage_free")
        u_stored = sem("u_stored")
        const_landed = sem("const_landed")
        const_ready = sem("const_ready")

        x_landed = [sem(f"x_landed{j}") for j in range(3)]
        tiles = range(KT)
        u_pe = Steps(sem("u_pe"), "bias rs " + " ".join(f"x{g}" for g in tiles))
        u_act = Steps(sem("u_act"), "sq0 sq1 sq2 root lb_e lam_e " + " ".join(f"x{g} h{g}" for g in tiles))
        u_vec = Steps(sem("u_vec"), "ones tab lb_max lb_d lam_p lam_d rs_inv rsb bias_vec rs "
                      + " ".join(f"h{g} l{g}" for g in tiles) + " lb_s lb_r lb omlb aT lam1 lam2 neg cf")
        u_pool = Steps(sem("u_pool"), "zero mean")
        x_kept = [sem(f"x_kept{j}") for j in range(2)]
        bias_stored = sem("bias_stored")
        head_landed = [sem(f"head_landed{j}") for j in range(2)]
        HEAD_LOADS = 16 * 9
        h_pe = Steps(sem("h_pe"), "scores vk i_t kd_t a ds pd_t pv ds_s o", 2)
        h_act = Steps(sem("h_act"), "ef lg eG tok p i_tok kd_tok pdt o_att", 2)
        h_vec = Steps(sem("h_vec"), "fg kin G Gd s max nmax qkd rc rcl pd2 pd own aT st1 st2 st3 st4 s_new o", 2)
        passed = sem("passed")
        h_pool = Steps(sem("h_pool"), "stored", 2)
        head_stored = sem("head_stored")
        k_turned, v_used = sem("k_turned"), sem("v_used")
        mix_landed = sem("mix_landed")
        s_n_landed, gate_landed, v_n_landed = sem("s_n_landed"), sem("gate_landed"), sem("v_n_landed")
        k_pe = Steps(sem("k_pe"), "ss s0 s1 s2 s3", 1)
        k_act = Steps(sem("k_act"), "q sq rt g0 silu g1 g2 g3 p", 1)
        k_vec = Steps(sem("k_vec"), "q rs on m0 rs_da silu da og m1 m2 near m3 mx nmx r w", 1)
        v_pe = Steps(sem("v_pe"), "t0 t1 new ot", 1)
        v_act = Steps(sem("v_act"), "h0 h1 o ot", 1)
        v_vec = Steps(sem("v_vec"), "l0 l1 o", 1)
        q_zero = sem("q_zero")
        d_pe = Steps(sem("d_pe"), "ss")
        d_act = Steps(sem("d_act"), "hh sq rt dh")
        d_vec = Steps(sem("d_vec"), "hl r n dl")
        b_act = Steps(sem("b_act"), "e hi")
        b_vec = Steps(sem("b_vec"), "yh yd sum lo")
        gates_landed, x_back = sem("gates_landed"), sem("x_back")
        m_act = Steps(sem("m_act"), "c0 c1 c2 c3 sq")
        m_vec = Steps(sem("m_vec"), "part sum", 1)
        e_pe = Steps(sem("e_pe"), "ss")
        e_act = Steps(sem("e_act"), "rt h0 sq0 h1 sq1 h2 sq2 h3 sq3 rt2")
        e_vec = Steps(sem("e_vec"), "rs n0 x0 l0 n1 x1 l1 n2 x2 l2 n3 x3 l3 rs2")
        e_pe2 = Steps(sem("e_pe2"), "p0 p1 p2 p3")
        f_act = Steps(sem("f_act"), "e")
        f_vec = Steps(sem("f_vec"), "g gs u act")
        down_done = sem("down_done")
        g_act = Steps(sem("g_act"), "c0 c1 c2 c3 c4 c5 c6 c7 q0 q1")
        g_vec = Steps(sem("g_vec"), "p0 s0 p1 s1")
        y_pe = Steps(sem("y_pe"), "ss " + " ".join(f"t{k}" for k in range(12)))
        y_act = Steps(sem("y_act"), "rt " + " ".join(f"o{k}" for k in range(12)))
        y_vec = Steps(sem("y_vec"), "rs n0 y0 n1 y1 n2 y2 n3 y3")
        sums_zero = sem("sums_zero")
        y_stored = sem("y_stored")
        block = ctx.enter_context(nc.Block())

        def w_granule(w, q, n):
            return w.rearrange("(q c p) n -> q p c n", c=2, p=P)[q][:, :, bass.ds(n * 512, 512)]

        def load(sp, r, slot, src, first=False):
            if not first:
                sp.wait_ge(lo_ready, r - RAW + 1)
            dst = raw[slot][:, :]
            if len(src.shape) == 3:
                dst = dst.rearrange("p (c n) -> p c n", c=2)
            sp.dma_start(dst, src).then_inc(raw_landed[slot], 16)

        def split_hi(act, r, slot, use, first=False):
            act.wait_ge(raw_landed[slot], 16 * use)
            if not first:
                act.wait_ge(granule_used, r - HALVES + 1)
            act.activation(w_hi[slot % HALVES][:, :], raw[slot][:, :], ACT.Copy).then_inc(hi_ready, 1)

        def split_lo(dve, r, slot):
            dve.wait_ge(hi_ready, r + 1)
            dve.tensor_tensor(w_lo[slot % HALVES][:, :], raw[slot][:, :],
                              w_hi[slot % HALVES][:, :].bitcast(F32), ALU.subtract).then_inc(lo_ready, 1)

        def products(pe, r, slot, xh, xl, bank, q, nq, free, by_bank=True):
            pe.wait_ge(lo_ready, r + 1)
            wh = w_hi[slot % HALVES][:, :].rearrange("p (c m k) -> p c m k", c=2, m=4)
            wl = w_lo[slot % HALVES][:, :].rearrange("p (c m k) -> p c m k", c=2, m=4)
            for m in range(4):
                if q == 0:
                    free(m)
                out = ps[:, bank + m, 0:T]
                for c in range(2):
                    first, last = q == 0 and c == 0, q == nq - 1 and c == 1
                    pe.matmul(out, wh[:, c, m, :], xh(c), start=first, stop=False)
                    pe.matmul(out, wl[:, c, m, :], xh(c), start=False, stop=False)
                    mm = pe.matmul(out, wh[:, c, m, :], xl(c), start=False, stop=last)
                if by_bank and q == nq - 1 and m < 3:
                    mm.then_inc(set_done, 1)
            mm.then_inc(granule_used, 1)

        def bank_ready(eng, s, m, r_end):
            if m < 3:
                eng.wait_ge(set_done, 3 * s + m + 1)
            else:
                eng.wait_ge(granule_used, r_end)

        NT = [(0, P), (P, P), (2 * P, CHUNK)]

        CONSTS = 16 * 12

        def head_loads(sp, h, par):
            sp.wait_ge(u_stored, 16 * (SETS_HEAD - 1) + 16 * h)
            sp.wait_ge(h_pe.sem, h_pe.last(h - 2))
            sp.wait_ge(h_vec.sem, h_vec.last(h - 2))
            sp.wait_ge(bias_stored, 16)
            sp.wait_ge(u_act.sem, u_act.last(0))
            sp.wait_ge(u_vec.sem, u_vec.last(0))
            for j in range(2):
                sp.wait_ge(x_kept[j], 32)
            done = head_landed[par]
            sp.dma_start(hin[par][:, :, :], uT[0:24].rearrange("(c h) p t -> h p c t", c=3)[
                bass.ds(h, 1)].rearrange("a p c t -> (a p) c t")).then_inc(done, 16)
            for dst, tile in ((mq, DQT), (mk, DKT)):
                rows = uT[tile:tile + 8].rearrange("(m c) (e d) t -> m (c e) d t", m=2, e=2)
                for m in range(2):
                    sp.dma_start(dst[par][DH * m:DH * m + DH, :],
                                 rows[m][bass.ds(h, 1)].rearrange("a d t -> (a d) t")).then_inc(done, 16)
            sp.dma_start(mv[par][:, :], uT[bass.ds(DVT + h, 1)].rearrange("a p t -> (a p) t")).then_inc(done, 16)
            sp.dma_start(s0[par][:, :, :], st.rearrange("b h p v -> h p b v")[
                bass.ds(h, 1)].rearrange("a p b v -> (a p) b v")).then_inc(done, 16)
            for m in range(2):
                skew = bass.AP(bias_rows.tensor, (h + 8 * m) * (P * BIAS_L) + P - 1,
                               [[BIAS_L - 1, P], [1, 2 * P]])
                sp.dma_start(mb[par][:, m, :], skew).then_inc(done, 16)

        def read_set(act, s, r_end, to):
            act.wait_ge(stage_free, s + 1)
            for m in range(4):
                bank_ready(act, s, m, r_end)
                act.activation(stage[to][:, m, :], ps[:, m, 0:T], ACT.Copy).then_inc(set_out, 1)

        def act_block(act, n, par, head=None):
            for q in range(8):
                split_hi(act, 8 * n + q, q, n + 1)
                if head and q != 1:
                    act_head(act, q, par, *head)
                if q == 1:
                    read_set(act, n - 1, 8 * n, 1 - par)
                    if head:
                        act_head(act, q, par, *head)

        def act_head(act, q, par, h, i):
            x = hin[par]
            if q == 0:
                h_act.begin()
                act.wait_ge(head_landed[par], HEAD_LOADS * (i + 1))
                act.wait_ge(h_vec.sem, h_vec.last(h - 1))
                act.wait_ge(h_pe.sem, h_pe.last(h - 1))
                act.wait_ge(h_pool.sem, h_pool.last(h - 1))
                act.wait_ge(h_act.sem, h_act.last(h - 1))
                h_act.done(act.activation(kin[:, :], x[:, 1, :], ACT.Sigmoid), "ef")
            if q == 1:
                act.wait_ge(h_vec.sem, h_vec.at(h, "fg"))
                h_act.done(act.activation(lg[:, :], fg[:, :], ACT.Ln), "lg")
            if q == 2:
                act.wait_ge(h_vec.sem, h_vec.at(h, "Gd"))
                act.activation(eG[:, :], G[:, :], ACT.Exp)
                act.activation(kg[:, :], G[:, :], ACT.Exp, scale=-1.0)
                h_act.done(act.activation(kd[:, :], lg[:, :], ACT.Exp), "eG")
                act.wait_ge(h_pe.sem, h_pe.at(h, "vk"))
                for bank, dst in ((6, v_tok), (7, k_tok)):
                    act.activation(dst[:, 0:2, :], ps[:, bank, 0:2 * P].rearrange("p (c d) -> p c d", c=2), ACT.Copy)
                    ins = act.activation(dst[0:CHUNK, 2, :], ps[0:CHUNK, bank, 2 * P:3 * P], ACT.Copy)
                h_act.done(ins, "tok")
            if q == 3:
                act.wait_ge(h_vec.sem, h_vec.at(h, "nmax"))
                for m in range(2):
                    for b, (c0, c1) in enumerate(((0, P), (P, 3 * P))):
                        k = 2 * m + b
                        ins = act.activation(s_at[:, m, c0:c1], s_at[:, m, c0:c1], ACT.Exp,
                                             bias=nmx[:, k:k + 1], accum_out=sm[:, k:k + 1])
                h_act.done(ins, "p")
                act.wait_ge(h_pe.sem, h_pe.at(h, "i_t"))
                act.activation(i_tok[:, 0:4, :], ps[0:CHUNK, 6, :].rearrange("p (c d) -> p c d", c=4), ACT.Copy)
                h_act.done(act.activation(i_tok[:, 4, :], ps[0:CHUNK, 7, 0:P], ACT.Copy), "i_tok")
            if q == 5:
                act.wait_ge(h_pe.sem, h_pe.at(h, "kd_t"))
                act.activation(kd_tok[:, 0:4, :], ps[0:CHUNK, 4, :].rearrange("p (c d) -> p c d", c=4), ACT.Copy)
                h_act.done(act.activation(kd_tok[:, 4, :], ps[0:CHUNK, 7, P:2 * P], ACT.Copy), "kd_tok")
            if q == 6:
                act.wait_ge(h_pe.sem, h_pe.at(h, "pd_t"))
                h_act.done(act.activation(pdt[:, :, :], ps[:, 6, 0:3 * P].rearrange("p (c d) -> p c d", c=3),
                                          ACT.Copy), "pdt")
            if q == 7:
                act.wait_ge(h_pe.sem, h_pe.at(h, "pv"))
                h_act.done(act.activation(o_da[:, bass.ds(h, 1), 0:SEQ].rearrange("p a t -> p (a t)"),
                                          ps[:, 5, 0:SEQ], ACT.Copy), "o_att")

        def vec_head(dve, q, par, h, i):
            def chain(ins, name):
                h_vec.done(ins, name)
                dve.wait_ge(h_vec.sem, h_vec.at(h, name))

            x = hin[par]
            if q == 0:
                h_vec.begin()
                dve.wait_ge(h_act.sem, h_act.at(h, "ef"))
                chain(dve.tensor_scalar(fg[:, :], kin[:, :], omlb[:, bass.ds(h, 1)], lb[:, bass.ds(h, 1)],
                                        ALU.mult, ALU.add), "fg")
                h_vec.done(dve.tensor_scalar(kin[:, :], fg[:, :], -1.0, 1.0, ALU.mult, ALU.add), "kin")
            if q == 1:
                dve.wait_ge(h_act.sem, h_act.at(h, "lg"))
                chain(dve.tensor_tensor_scan(G[:, :], scan_keep[:, :], lg[:, :], 0.0, ALU.mult, ALU.add), "G")
                for t0, k, n in ((0, SEQ // CHUNK, CHUNK), (SEQ, NB, NQ)):
                    g = G[:, t0:t0 + k * n].rearrange("p (k n) -> p k n", n=n)
                    ins = dve.tensor_tensor(lg[:, t0:t0 + k * n].rearrange("p (k n) -> p k n", n=n),
                                            g[:, :, n - 1:n].broadcast_to([P, k, n]), g, ALU.subtract)
                h_vec.done(ins, "Gd")
            if q == 2:
                dve.wait_ge(h_pe.sem, h_pe.at(h, "scores"))
                for m in range(2):
                    near = mb[par][:, m, :]
                    dve.scalar_tensor_tensor(s_at[:, m, 0:P], ps[:, 4 + m, 0:P], SCALE, near[:, P:2 * P],
                                             ALU.mult, ALU.add)
                    dve.scalar_tensor_tensor(s_at[:, m, P:3 * P], ps[:, 4 + m, P:3 * P], SCALE, near,
                                             ALU.mult, ALU.add)
                    ins = dve.tensor_scalar(s_sm[:, m, :], ps[0:CHUNK, 4 + m, 3 * P:3 * P + CHUNK], SCALE,
                                            None, ALU.mult)
                chain(ins, "s")
                for m in range(2):
                    dve.tensor_reduce(mx[:, 2 * m:2 * m + 1], s_at[:, m, 0:P], AX_X, ALU.max)
                    ins = dve.tensor_reduce(mx[:, 2 * m + 1:2 * m + 2], s_at[:, m, P:3 * P], AX_X, ALU.max)
                chain(ins, "max")
                h_vec.done(dve.tensor_scalar(nmx[:, :], mx[:, :], -1.0, None, ALU.mult), "nmax")
            if q == 3:
                dve.wait_ge(h_act.sem, h_act.at(h, "eG"))
                dve.tensor_tensor(qg[:, :], x[:, 0, :], eG[:, :], ALU.mult)
                dve.tensor_tensor(kg[:, :], kg[:, :], kin[:, :], ALU.mult)
                h_vec.done(dve.tensor_tensor(kd[:, :], kd[:, :], kin[:, :], ALU.mult), "qkd")
            if q == 4:
                dve.wait_ge(h_act.sem, h_act.at(h, "p"))
                chain(dve.reciprocal(rc[:, :], sm[:, :]), "rc")
                chain(dve.tensor_scalar(rc[:, 2:4], rc[:, 2:4], neg_lam[:, 0:1], None, ALU.mult), "rcl")
                spans = ((0, P), (P, 3 * P))
                for b, (c0, c1) in enumerate(spans):
                    ins = dve.tensor_scalar(pd2[:, c0:c1], s_at[:, 1, c0:c1], rc[:, 2 + b:3 + b], None, ALU.mult)
                chain(ins, "pd2")
                for b, (c0, c1) in enumerate(spans):
                    ins = dve.scalar_tensor_tensor(pd[:, c0:c1], s_at[:, 0, c0:c1], rc[:, b:b + 1],
                                                   pd2[:, c0:c1], ALU.mult, ALU.add)
                h_vec.done(ins, "pd")
            if q == 5:
                dve.wait_ge(h_act.sem, h_act.at(h, "i_tok"))
                h_vec.done(dve.tensor_tensor(
                    i_own[:, :, :], i_tok[:, 4:5, :].broadcast_to([CHUNK, NB, DV]),
                    own[:, :].unsqueeze(2).broadcast_to([CHUNK, NB, DV]), ALU.mult), "own")
                dve.wait_ge(h_pe.sem, h_pe.at(h, "a"))
                dve.sem_inc(passed, 1)
                h_vec.done(dve.copy_predicated(aT[:, :, :].rearrange("p c n -> p (c n)"),
                                               causal[:, :, :].rearrange("p c n -> p (c n)"),
                                               ps[0:CHUNK, 5, 0:T]), "aT")
            if q == 6:
                dve.wait_ge(h_pe.sem, h_pe.at(h, "ds"))
                chain(dve.tensor_copy(state[:, 0, :], ps[:, 4, 0:DV]), "st1")
                for c in range(1, 4):
                    last = CHUNK * c + CHUNK - 1
                    ins = dve.scalar_tensor_tensor(state[:, c, :], state[:, c - 1, :], eG[:, last:last + 1],
                                                   ps[:, 4, c * DV:(c + 1) * DV], ALU.mult, ALU.add)
                    chain(ins, f"st{c + 1}")
            if q == 7:
                dve.wait_ge(h_pe.sem, h_pe.at(h, "ds_s"))
                for b in range(NB):
                    last = SEQ + NQ * b + NQ - 1
                    ins = dve.scalar_tensor_tensor(s_new[:, b, :], s0[par][:, b, :], eG[:, last:last + 1],
                                                   ps[:, 6 + b // 4, b % 4 * DV:(b % 4 + 1) * DV],
                                                   ALU.mult, ALU.add)
                h_vec.done(ins, "s_new")
                dve.wait_ge(h_pe.sem, h_pe.at(h, "o"))
                h_vec.done(dve.tensor_copy(o_hg[:, bass.ds(h, 1), :].rearrange("p a t -> p (a t)"),
                                           ps[:, 4, 0:T]), "o")

        def pe_head(pe, q, par, h, i):
            x, seq = hin[par], range(SEQ // CHUNK)
            span = [slice(CHUNK * c, CHUNK * (c + 1)) for c in range(CHUNKS)]

            def five(src, bank, col):
                pe.sem_inc(passed, 1)
                for c in range(CHUNKS):
                    out = ps[0:CHUNK, bank, c * P:(c + 1) * P] if c < 4 else ps[0:CHUNK, 7, col:col + P]
                    ins = pe.transpose(out, src[:, span[c]], ident[:, :])
                return ins

            if q == 0:
                h_pe.begin()
                pe.wait_ge(head_landed[par], HEAD_LOADS * (i + 1))
                pe.wait_ge(h_act.sem, h_act.last(h - 1))
                pe.wait_ge(h_vec.sem, h_vec.last(h - 1))
                for m in range(2):
                    own_q, own_k = mq[par][DH * m:DH * m + DH, :], mk[par][DH * m:DH * m + DH, :]
                    pe.matmul(ps[:, 4 + m, 0:P], own_q[:, 0:P], own_k[:, 0:P], start=True, stop=True)
                    pe.matmul(ps[:, 4 + m, P:3 * P], own_q[:, P:SEQ], own_k[:, 0:SEQ], start=True, stop=True)
                    ins = pe.matmul(ps[0:CHUNK, 4 + m, 3 * P:3 * P + CHUNK], own_q[:, SEQ:T], own_k[:, SEQ:T],
                                    start=True, stop=True)
                h_pe.done(ins, "scores")
                for bank, src in ((6, mv), (7, mk)):
                    for j, (t0, n) in enumerate(NT):
                        ins = pe.transpose(ps[0:n, bank, j * P:(j + 1) * P], src[par][:, t0:t0 + n], ident[:, :])
                h_pe.done(ins, "vk")
            if q == 1:
                pe.wait_ge(h_act.sem, h_act.at(h, "tok"))
                h_pe.done(five(x[:, 2, :], 6, 0), "i_t")
            if q == 3:
                pe.wait_ge(h_vec.sem, h_vec.at(h, "qkd"))
                pe.wait_ge(h_act.sem, h_act.at(h, "i_tok"))
                h_pe.done(five(kd, 4, P), "kd_t")
                for c in range(CHUNKS):
                    ins = pe.matmul(ps[0:CHUNK, 5, span[c]], kg[:, span[c]], qg[:, span[c]], start=True, stop=True)
                h_pe.done(ins, "a")
            if q == 4:
                pe.wait_ge(h_act.sem, h_act.at(h, "kd_tok"))
                for c in seq:
                    ins = pe.matmul(ps[:, 4, c * DV:(c + 1) * DV], kd_tok[:, c, :], i_tok[:, c, :],
                                    start=True, stop=True)
                h_pe.done(ins, "ds")
                pe.wait_ge(h_vec.sem, h_vec.at(h, "pd"))
                for j in range(3):
                    ins = pe.transpose(ps[:, 6, j * P:(j + 1) * P], pd[:, j * P:(j + 1) * P], ident[:, :])
                h_pe.done(ins, "pd_t")
            if q == 5:
                pe.wait_ge(h_act.sem, h_act.at(h, "pdt"))
                pe.wait_ge(h_vec.sem, h_vec.at(h, "aT"))
                pe.matmul(ps[:, 5, 0:P], v_tok[:, 0, :], pdt[:, 0, :], start=True, stop=True)
                pe.matmul(ps[:, 5, P:2 * P], v_tok[:, 0, :], pdt[:, 1, :], start=True, stop=False)
                h_pe.done(pe.matmul(ps[:, 5, P:2 * P], v_tok[:, 1, :], pdt[:, 2, :], start=False, stop=True), "pv")
                for k in range(2):
                    ins = pe.matmul(ps[:, 6 + k, :], kd_tok[:, 4, :], i_own[:, 4 * k:4 * k + 4, :],
                                    start=True, stop=True)
                h_pe.done(ins, "ds_s")
            if q == 6:
                pe.wait_ge(h_vec.sem, h_vec.at(h, "st4"))
                for c in seq:
                    pe.matmul(ps[:, 4, span[c]], i_tok[:, c, :], aT[:, c, :], start=True, stop=c == 0)
                    if c:
                        pe.matmul(ps[:, 4, span[c]], state[:, c - 1, :], qg[:, span[c]], start=False, stop=True)
                pe.matmul(ps[:, 4, span[4]], i_tok[:, 4, :], aT[:, 4, :], start=True, stop=True)
                for b in range(NB):
                    t0 = SEQ + NQ * b
                    ins = pe.matmul(ps[:, 4, t0:t0 + NQ], s0[par][:, b, :], qg[:, t0:t0 + NQ],
                                    start=False, stop=True, skip_group_check=True)
                h_pe.done(ins, "o")

        def store_set(pool, s, at):
            pool.wait_ge(set_out, 4 * s + 4)
            pool.dma_start(uT[bass.ds(4 * s, 4)].rearrange("c p t -> p c t"), stage[at][:, :, :]).then_inc(u_stored, 16)
            pool.wait_ge(u_stored, 16 * s + 16)
            pool.sem_inc(stage_free, 1)

        HEAD_STORES = 16 * 9

        def pool_head(pool, par, h):
            def two(a):
                return a.rearrange("(c p) d -> p c d", p=P)

            one = bass.ds(h, 1)
            pool.wait_ge(h_act.sem, h_act.at(h, "tok"))
            kp = k_p.rearrange("t (m h) d -> m h t d", m=2)
            ks = k_s.rearrange("t (m h) d -> m h t d", m=2)
            for m in range(2):
                c = slice(DH * m, DH * m + DH)
                pool.dma_start(two(kp[m][one].rearrange("a t d -> (a t) d")), k_tok[:, 0:2, c]).then_inc(head_stored, 16)
                pool.dma_start(ks[m][one].rearrange("a t d -> (a t) d"), k_tok[0:CHUNK, 2, c]).then_inc(head_stored, 16)
            pool.dma_start(two(v_p.rearrange("t h d -> h t d")[one].rearrange("a t d -> (a t) d")),
                           v_tok[:, 0:2, :]).then_inc(head_stored, 16)
            pool.dma_start(v_s.rearrange("t h d -> h t d")[one].rearrange("a t d -> (a t) d"),
                           v_tok[0:CHUNK, 2, :]).then_inc(head_stored, 16)
            pool.wait_ge(h_vec.sem, h_vec.at(h, "s"))
            pool.dma_start(new_scores.rearrange("(m h) q k -> h q m k", m=2)[one].rearrange("a q m k -> (a q) m k"),
                           s_sm[:, :, :]).then_inc(head_stored, 16)
            pool.wait_ge(h_vec.sem, h_vec.at(h, "s_new"))
            pool.dma_start(h_p[one].rearrange("a p v -> (a p) v"), state[:, 3, :]).then_inc(head_stored, 16)
            pool.dma_start(h_s.rearrange("b h p v -> h p b v")[one].rearrange("a p b v -> (a p) b v"),
                           s_new[:, :, :]).then_inc(head_stored, 16)
            pool.wait_ge(head_stored, HEAD_STORES * (h + 1))
            pool.sem_inc(h_pool.sem, 1)

        def order(has_k, has_v):
            if not (has_k and has_v):
                return [("K" if has_k else "V", p) for p in range(PAGES)]
            out = [("K", p) for p in range(4)] + [("V", 0)]
            for p in range(4, PAGES):
                out += [("V", p - 3), ("K", p)]
            return out + [("V", p) for p in range(PAGES - 3, PAGES)]

        def mix_r(n, has_k, has_v, what):
            at = order(has_k, has_v).index(what)
            past = 0 if not has_v else PAGES + 2 * PAGES * (n - 1)
            use = R_MIX // RAW + (0 if not has_v else PAGES // RAW + 2 * PAGES // RAW * (n - 1))
            return R_MIX + past + at, at % RAW, use + at // RAW + 1

        def rounds(eng, do):
            do(eng, 0, True, False)
            with eng.Fori(1, NB) as n:
                do(eng, n, True, True)
            do(eng, NB, False, True)

        def heads_of(t, d, step):
            return bass.AP(t.tensor, t.offset + d, [list(t.ap[0]), [step, 8], [1, NQ]])

        def sync_mix(sp, n, has_k, has_v):
            if not has_v:
                sp.wait_ge(const_landed, CONSTS)
            for kind, p in order(has_k, has_v):
                r, slot, _ = mix_r(n, has_k, has_v, (kind, p))
                cache, b = (ck, n) if kind == "K" else (cv, n - 1)
                page = sp.value_load(pages[0:1, bass.ds(b * PAGES + p, 1)], min_val=0, max_val=POOL - 1)
                load(sp, r, slot, cache[bass.ds(page, 1)].rearrange("a p n -> (a p) n"))

        def turned(t, p):
            return t[p // 4 % 2][:, :, p % 4 * PAGE:(p % 4 + 1) * PAGE]

        def bank_pair(p):
            return ps[:, p % 2 * 2:p % 2 * 2 + 2, :].rearrange("p b n -> p (b n)").rearrange(
                "p (c k) -> p c k", c=8)

        def act_mix(act, n, has_k, has_v):
            b = n - 1
            k_act.begin()
            v_act.begin()

            def value_hi(j):
                r, slot, use = mix_r(n, has_k, has_v, ("V", j))
                act.wait_ge(raw_landed[slot], 16 * use)
                act.wait_ge(v_used, PAGES * b + j + 1)
                act.activation(w_hi[j % HALVES][:, :], raw[slot][:, :], ACT.Copy).then_inc(hi_ready, 1)

            def group(g):
                act.wait_ge(k_pe.sem, k_pe.at(n, f"s{g}"))
                w = 4 * PAGE if g < 3 else 3 * PAGE
                k_act.done(act.activation(s_all[:, g * 4 * PAGE:g * 4 * PAGE + w], ps[:, 4 + g % 2, 0:w],
                                          ACT.Identity, bias=far[:, 0:1]), f"g{g}")

            for p in range(PAGES):
                if p == 12 and not has_k:
                    act.wait_ge(k_vec.sem, k_vec.at(NB - 1, "og"))
                    act.wait_ge(k_pe.sem, k_pe.last(NB - 1))
                    for e in range(2):
                        ins = act.activation(br_hi[0][:, half[e], :], o_hg[:, half[e], :], ACT.Copy)
                    d_act.done(ins, "hh")
                if has_v and p == 4:
                    value_hi(0)
                if has_v and p >= 4:
                    value_hi(p - 3)
                if has_k:
                    r, _, _ = mix_r(n, has_k, has_v, ("K", p))
                    act.wait_ge(k_turned, PAGES * n + p + 1)
                    act.activation(turned(kt_hi, p), bank_pair(p), ACT.Copy).then_inc(hi_ready, 1)
                    if p == 2:
                        act.wait_ge(k_pe.sem, k_pe.at(n - 1, "s3"))
                        act.wait_ge(mix_landed, MIX_LOADS)
                        for m in range(2):
                            own = slice(DH * m, DH * m + DH)
                            ins = act.activation(heads_of(q_hi[own, :, :], NQ * m, P + 2 * NQ),
                                                 q_all[own, :, bass.ds(NQ * n, NQ)], ACT.Copy, scale=SCALE)
                        k_act.done(ins, "q")
                        act.activation(n_sq, o_hg[:, bass.ds(n, 1), :].rearrange("p a t -> p (a t)"), ACT.Square)
                        k_act.done(act.activation(n_sq2, o_da[:, bass.ds(n, 1), 0:SEQ].rearrange("p a t -> p (a t)"),
                                                  ACT.Square), "sq")
                    if p == 4:
                        act.wait_ge(k_pe.sem, k_pe.at(n, "ss"))
                        act.wait_ge(k_vec.sem, k_vec.at(n - 1, "og"))
                        act.activation(n_rs, ps[:, 5, 0:T], ACT.Sqrt, scale=1.0 / DV, bias=eps_c[:, 0:1])
                        k_act.done(act.activation(n_rs2, ps[:, 4, 0:SEQ], ACT.Sqrt, scale=1.0 / DV,
                                                  bias=eps_c[:, 0:1]), "rt")
                    if p == 8:
                        act.wait_ge(gate_landed, 16 * (n + 1))
                        k_act.done(act.activation(n_e, n_gate, ACT.Sigmoid), "silu")
                    if p in (6, 10, 14):
                        if p == 6:
                            act.wait_ge(k_vec.sem, k_vec.at(n - 1, "w"))
                        group((p - 6) // 4)
                if has_v and p < 2:
                    j = p
                    act.wait_ge(v_pe.sem, v_pe.at(b, f"t{j}"))
                    ins = act.activation(p_hi[:, 8 * j:8 * j + 8, :], ps[:, 4:6, :].rearrange(
                        "p b n -> p (b n)").rearrange("p (c k) -> p c k", c=8), ACT.Copy)
                    if j:
                        ins = act.activation(p_new[:, :], ps[0:NQ, 6, 0:P], ACT.Copy)
                    v_act.done(ins, f"h{j}")
            if has_v:
                for j in range(PAGES - 3, PAGES):
                    value_hi(j)
            if has_k:
                group(3)
            if has_k:
                act.wait_ge(k_vec.sem, k_vec.at(n, "nmx"))
                k_act.done(act.activation(s_all[:, :], s_all[:, :], ACT.Exp, bias=mxk[:, 5:6],
                                          accum_out=l_all[:, 0:1]), "p")
            if has_v:
                act.wait_ge(v_pe.sem, v_pe.at(b, "new"))
                v_act.done(act.activation(o_rows[:, :], ps[:, 6:8, :].rearrange("p b n -> p (b n)"),
                                          ACT.Copy, scale=w_row[:, 0:1]), "o")
                act.wait_ge(v_pe.sem, v_pe.at(b, "ot"))
                v_act.done(act.activation(o_second[:, :, :], heads_of(ps[:, 4:6, :], 64, P + NQ), ACT.Copy), "ot")

        def vec_mix(dve, n, has_k, has_v):
            b = n - 1
            k_vec.begin()
            v_vec.begin()

            def chain(ins, name):
                k_vec.done(ins, name)
                dve.wait_ge(k_vec.sem, k_vec.at(n, name))

            def value_lo(j):
                r, slot, _ = mix_r(n, has_k, has_v, ("V", j))
                dve.wait_ge(hi_ready, r + 1)
                dve.tensor_tensor(w_lo[j % HALVES][:, :], raw[slot][:, :], w_hi[j % HALVES][:, :].bitcast(F32),
                                  ALU.subtract).then_inc(lo_ready, 1)

            for p in range(PAGES):
                if p == 12 and not has_k:
                    dve.wait_ge(d_act.sem, d_act.at(0, "hh"))
                    for e in range(2):
                        ins = dve.tensor_tensor(br_lo[0][:, half[e], :], o_hg[:, half[e], :],
                                                br_hi[0][:, half[e], :].bitcast(F32), ALU.subtract)
                    d_vec.done(ins, "hl")
                if has_v and p == 4:
                    value_lo(0)
                if has_v and p >= 4:
                    value_lo(p - 3)
                if has_k:
                    r, _, _ = mix_r(n, has_k, has_v, ("K", p))
                    dve.wait_ge(hi_ready, r + 1)
                    dve.tensor_tensor(turned(kt_lo, p), bank_pair(p), turned(kt_hi, p).bitcast(F32),
                                      ALU.subtract).then_inc(lo_ready, 1)
                    if p == 3:
                        dve.wait_ge(k_act.sem, k_act.at(n, "q"))
                        for m in range(2):
                            own = slice(DH * m, DH * m + DH)
                            ins = dve.scalar_tensor_tensor(
                                heads_of(q_lo[own, :, :], NQ * m, P + 2 * NQ), q_all[own, :, bass.ds(NQ * n, NQ)],
                                SCALE, heads_of(q_hi[own, :, :].bitcast(F32), NQ * m, P + 2 * NQ), ALU.mult, ALU.subtract)
                        k_vec.done(ins, "q")
                    o = o_hg[:, bass.ds(n, 1), :].rearrange("p a t -> p (a t)")
                    o2 = o_da[:, bass.ds(n, 1), 0:SEQ].rearrange("p a t -> p (a t)")
                    if p == 5:
                        dve.wait_ge(k_act.sem, k_act.at(n, "rt"))
                        k_vec.done(dve.reciprocal(n_rs, n_rs), "rs")
                    if p == 6:
                        dve.wait_ge(k_vec.sem, k_vec.at(n, "rs"))
                        k_vec.done(dve.scalar_tensor_tensor(o, o, hg_w[:, 0:1], n_rs, ALU.mult, ALU.mult), "on")
                    if p == 8:
                        k_vec.done(dve.reciprocal(n_rs2, n_rs2), "rs_da")
                    if p == 9:
                        dve.wait_ge(k_act.sem, k_act.at(n, "silu"))
                        chain(dve.tensor_tensor(n_e, n_e, n_gate, ALU.mult), "silu")
                        k_vec.done(dve.scalar_tensor_tensor(o2, o2, hg_w[:, 1:2], n_rs2, ALU.mult, ALU.mult), "da")
                        k_vec.done(dve.tensor_tensor(o, o, n_e, ALU.mult), "og")
                    if p in (6, 10, 14):
                        g = (p - 6) // 4
                        dve.wait_ge(k_act.sem, k_act.at(n, f"g{g}"))
                        k_vec.done(dve.tensor_reduce(mxk[:, g:g + 1], s_all[:, g * 4 * PAGE:(g + 1) * 4 * PAGE],
                                                     AX_X, ALU.max), f"m{g}")
                if has_v and p < 2:
                    j = p
                    dve.wait_ge(v_act.sem, v_act.at(b, f"h{j}"))
                    v_vec.done(dve.tensor_tensor(
                        p_lo[:, 8 * j:8 * j + 8, :],
                        ps[:, 4:6, :].rearrange("p b n -> p (b n)").rearrange("p (c k) -> p c k", c=8),
                        p_hi[:, 8 * j:8 * j + 8, :].bitcast(F32), ALU.subtract), f"l{j}")
            if has_v:
                for j in range(PAGES - 3, PAGES):
                    value_lo(j)
            if has_k:
                dve.wait_ge(k_act.sem, k_act.at(n, "g3"))
                dve.wait_ge(s_n_landed, 16 * (n + 1))
                dve.tensor_tensor(s_all[:, PAST - PAGE:PAST], ps[:, 5, 3 * PAGE:4 * PAGE], near[:, 0:PAGE], ALU.add)
                chain(dve.tensor_tensor(s_all[:, PAST:], s_n[:, :], near[:, PAGE:], ALU.add), "near")
                chain(dve.tensor_reduce(mxk[:, 3:4], s_all[:, 12 * PAGE:], AX_X, ALU.max), "m3")
                chain(dve.tensor_reduce(mxk[:, 4:5], mxk[:, 0:4], AX_X, ALU.max), "mx")
                k_vec.done(dve.tensor_scalar(mxk[:, 5:6], mxk[:, 4:5], -1.0, None, ALU.mult), "nmx")
            if has_v:
                dve.wait_ge(v_act.sem, v_act.at(b, "ot"))
                v_vec.done(dve.tensor_tensor(o_da[:, :, bass.ds(SEQ + NQ * b, NQ)], o_second[:, :, :],
                                             heads_of(ps[:, 4:6, :], 0, P + NQ), ALU.add), "o")
            if has_k:
                dve.wait_ge(k_act.sem, k_act.at(n, "p"))
                chain(dve.reciprocal(l_all[:, 1:2], l_all[:, 0:1]), "r")
                k_vec.done(dve.tensor_tensor(w_row[:, :], l_all[:, 1:2], cf[:, :], ALU.mult), "w")

        def pe_mix(pe, n, has_k, has_v):
            b = n - 1
            k_pe.begin()
            v_pe.begin()

            def value(j):
                r, _, _ = mix_r(n, has_k, has_v, ("V", j))
                pe.wait_ge(lo_ready, r + 1)
                if j == 0:
                    pe.wait_ge(v_vec.sem, v_vec.at(b, "l1"))
                wh, wl = w_hi[j % HALVES], w_lo[j % HALVES]
                for k in range(2):
                    c = slice(512 * k, 512 * k + 512)
                    pe.matmul(ps[:, 6 + k, :], p_hi[:, j, :], wh[:, c], start=j == 0, stop=False)
                    pe.matmul(ps[:, 6 + k, :], p_lo[:, j, :], wh[:, c], start=False, stop=False)
                    ins = pe.matmul(ps[:, 6 + k, :], p_hi[:, j, :], wl[:, c], start=False, stop=False)
                ins.then_inc(v_used, 1)

            def scores(g):
                r, _, _ = mix_r(n, has_k, has_v, ("K", 4 * g + 3))
                pe.wait_ge(lo_ready, r + 1)
                if g == 0:
                    pe.wait_ge(k_vec.sem, k_vec.at(n, "q"))
                    pe.wait_ge(k_act.sem, k_act.at(n, "rt"))
                if g >= 2:
                    pe.wait_ge(k_act.sem, k_act.at(n, f"g{g - 2}"))
                out, kh, kl = ps[:, 4 + g % 2, :], kt_hi[g % 2], kt_lo[g % 2]
                for c in range(8):
                    pe.matmul(out, q_hi[:, c, :], kh[:, c, :], start=c == 0, stop=False)
                    pe.matmul(out, q_lo[:, c, :], kh[:, c, :], start=False, stop=False)
                    ins = pe.matmul(out, q_hi[:, c, :], kl[:, c, :], start=False, stop=c == 7)
                k_pe.done(ins, f"s{g}")

            for p in range(PAGES):
                if has_k:
                    r, slot, use = mix_r(n, has_k, has_v, ("K", p))
                    pe.wait_ge(raw_landed[slot], 16 * use)
                    if p >= 2:
                        pe.wait_ge(lo_ready, mix_r(n, has_k, has_v, ("K", p - 2))[0] + 1)
                    else:
                        pe.wait_ge(lo_ready, mix_r(n, has_k, has_v, ("K", 0))[0])
                    for c in range(8):
                        ins = pe.transpose(bank_pair(p)[:, c, :], raw[slot][:, c * P:(c + 1) * P], ident[:, :])
                    ins.then_inc(k_turned, 1)
                    if p == 3:
                        pe.wait_ge(k_act.sem, k_act.at(n, "sq"))
                        if has_v:
                            pe.wait_ge(v_vec.sem, v_vec.at(b, "l1"))
                        else:
                            pe.wait_ge(h_act.sem, h_act.last(HEADS - 1))
                            pe.wait_ge(h_vec.sem, h_vec.last(HEADS - 1))
                        pe.matmul(ps[:, 5, 0:T], ones[:, :], n_sq, start=True, stop=True)
                        k_pe.done(pe.matmul(ps[:, 4, 0:SEQ], ones[:, :], n_sq2, start=True, stop=True), "ss")
                    if p > 4 and p % 4 == 1:
                        scores(p // 4 - 1)
                if has_v and p < 2:
                    j = p
                    if j == 0:
                        pe.wait_ge(k_act.sem, k_act.at(b, "p"))
                        pe.wait_ge(v_vec.sem, v_vec.at(b - 1, "o"))
                    else:
                        pe.wait_ge(v_vec.sem, v_vec.at(b, "l0"))
                    for c in range(8):
                        t = 8 * j + c
                        ins = pe.transpose(ps[:, 4 + c // 4, c % 4 * P:(c % 4 + 1) * P],
                                           s_all[:, t * PAGE:(t + 1) * PAGE], ident[:, :])
                    if j:
                        ins = pe.transpose(ps[0:NQ, 6, 0:P], s_all[:, PAST:], ident[:, :])
                    v_pe.done(ins, f"t{j}")
                if has_v and p >= 4:
                    value(p - 4)
            if has_v:
                value(PAGES - 4)
            if has_k:
                scores(3)
            if has_v:
                for j in range(PAGES - 3, PAGES):
                    value(j)
                pe.wait_ge(v_n_landed, 16 * n)
                for k in range(2):
                    ins = pe.matmul(ps[:, 6 + k, :], p_new[:, :], v_new[:, 512 * k:512 * k + 512],
                                    start=False, stop=True)
                v_pe.done(ins, "new")
                pe.wait_ge(v_act.sem, v_act.at(b, "o"))
                if has_k:
                    pe.wait_ge(k_vec.sem, k_vec.at(n, "near"))
                for h in range(HEADS):
                    ins = pe.transpose(ps[:, 4 + h // 4, h % 4 * P:(h % 4 + 1) * P],
                                       o_rows[:, h * DV:(h + 1) * DV], ident[:, :])
                v_pe.done(ins, "ot")

        def pool_mix(pool, n, has_k, has_v):
            if has_k:
                pool.wait_ge(k_vec.sem, k_vec.at(n - 1, "near"))
                src = bass.AP(new_scores.tensor, (NB * NQ + 1) * NQ * n,
                              [[(NB * NQ) ** 2, MAPS], [NB * NQ, NQ], [1, NQ]])
                pool.dma_start(s_n[:, :], src).then_inc(s_n_landed, 16)
                pool.wait_ge(k_vec.sem, k_vec.at(n - 1, "og"))
                pool.dma_start(n_gate, uT[bass.ds(OT + n, 1)].rearrange("a p t -> (a p) t")).then_inc(gate_landed, 16)
            if has_v:
                pool.wait_ge(v_pe.sem, v_pe.at(n - 2, "new"))
                pool.dma_start(v_new[:, :], v_s.rearrange("(b q) h d -> b q (h d)", q=NQ)[
                    bass.ds(n - 1, 1)].rearrange("a q d -> (a q) d")).then_inc(v_n_landed, 16)

        MIX_LOADS = 16 * 3

        BLOCKS = D_MODEL // 512
        half = [slice(0, 4), slice(4, 8)]
        s_flat = stage[0][:, :, :].rearrange("p m t -> p (m t)")[:, 0:HEADS * NB * NQ]

        def branch_w(j, q):
            return w_granule(w_hg if q < 4 else w_da, q % 4, j)

        def act_branch(act, j, first=False):
            for q in range(8):
                r = R_BRANCH + 8 * j + q
                split_hi(act, r, q, r_use(R_BRANCH + q) + j)
                if first and q == 1:
                    act.wait_ge(d_pe.sem, d_pe.at(0, "ss"))
                    d_act.done(act.activation(s_flat, ps[:, 4, :], ACT.Sqrt, scale=1.0 / DV, bias=eps_c[:, 0:1]), "rt")
                if first and q == 2:
                    act.wait_ge(d_vec.sem, d_vec.at(0, "n"))
                    for b in range(2):
                        ins = act.activation(br_hi[1][:, half[b], :], o_da[:, half[b], :], ACT.Copy,
                                             scale=1.0 - LAM_INIT)
                    d_act.done(ins, "dh")
                if not first and q == 2:
                    act_merged(act, j - 1)
                if q == 3:
                    b_act.begin()
                    act.wait_ge(gates_landed, 32 * (j + 1))
                    b_act.done(act.activation(gates[:, :, :, :], gates[:, :, :, :], ACT.Sigmoid), "e")

        def act_merged(act, j):
            act.wait_ge(b_vec.sem, b_vec.at(j, "sum"))
            b_act.done(act.activation(m_hi[:, bass.ds(4 * j, 4), :], stage[0][:, :, :], ACT.Copy), "hi")

        def vec_branch(dve, j, first=False):
            def chain(ins, name, st=b_vec, rnd=j):
                st.done(ins, name)
                dve.wait_ge(st.sem, st.at(rnd, name))

            for q in range(8):
                r = R_BRANCH + 8 * j + q
                split_lo(dve, r, q)
                if first and q == 1:
                    dve.wait_ge(d_act.sem, d_act.at(0, "rt"))
                    chain(dve.reciprocal(s_flat, s_flat), "r", d_vec, 0)
                    chain(dve.scalar_tensor_tensor(
                        o_da[:, :, SEQ:], o_da[:, :, SEQ:], hg_w[:, 1:2], s_flat.rearrange("p (h t) -> p h t", h=HEADS),
                        ALU.mult, ALU.mult), "n", d_vec, 0)
                if first and q == 2:
                    dve.wait_ge(d_act.sem, d_act.at(0, "dh"))
                    for b in range(2):
                        ins = dve.scalar_tensor_tensor(br_lo[1][:, half[b], :], o_da[:, half[b], :],
                                                       1.0 - LAM_INIT, br_hi[1][:, half[b], :].bitcast(F32),
                                                       ALU.mult, ALU.subtract)
                    chain(ins, "dl", d_vec, 0)
                if not first and q == 1:
                    vec_merge(dve, j - 1)
                if not first and q == 2:
                    vec_merged(dve, j - 1)
                if q == 5:
                    b_vec.begin()
                    dve.wait_ge(b_act.sem, b_act.at(j, "e"))
                    dve.wait_ge(granule_used, R_BRANCH + 8 * j + 4)
                    if not first:
                        dve.wait_ge(b_vec.sem, b_vec.at(j - 1, "lo"))
                    b_vec.done(dve.tensor_tensor(stage[0][:, :, :], ps[:, 0:4, 0:T], gates[:, 0], ALU.mult), "yh")

        def vec_merge(dve, j):
            dve.wait_ge(granule_used, R_BRANCH + 8 * j + 8)
            b_vec.done(dve.tensor_tensor(stage[1][:, :, :], ps[:, 4:8, 0:T], gates[:, 1], ALU.mult), "yd")
            dve.wait_ge(b_vec.sem, b_vec.at(j, "yd"))
            b_vec.done(dve.tensor_tensor(stage[0][:, :, :], stage[0][:, :, :], stage[1][:, :, :], ALU.add), "sum")

        def vec_merged(dve, j):
            dve.wait_ge(b_act.sem, b_act.at(j, "hi"))
            b_vec.done(dve.tensor_tensor(m_lo[:, bass.ds(4 * j, 4), :], stage[0][:, :, :],
                                         m_hi[:, bass.ds(4 * j, 4), :].bitcast(F32), ALU.subtract), "lo")

        def pe_branch(pe, j, first=False):
            for q in range(8):
                r = R_BRANCH + 8 * j + q
                b = q // 4
                if first and q == 0:
                    pe.wait_ge(d_vec.sem, d_vec.at(0, "hl"))
                if first and q == 1:
                    pe.wait_ge(d_act.sem, d_act.at(0, "sq"))
                    d_pe.done(pe.matmul(ps[:, 4, :], ones[:, :], s_flat, start=True, stop=True), "ss")
                if first and q == 4:
                    pe.wait_ge(d_vec.sem, d_vec.at(0, "dl"))

                def free(m):
                    if m == 0 and not first:
                        pe.wait_ge(b_vec.sem, b_vec.at(j - 1, "yd" if b else "yh"))

                products(pe, r, q, lambda c: br_hi[b][:, 2 * (q % 4) + c, :], lambda c: br_lo[b][:, 2 * (q % 4) + c, :],
                         4 * b, q % 4, 4, free, by_bank=False)

        def pool_branch(pool, j, first=False):
            if not first:
                pool.wait_ge(b_vec.sem, b_vec.at(j - 1, "yd"))
            for b, tile in enumerate((GHT, GDT)):
                pool.dma_start(gates[:, b], uT[tile:tile + 16].rearrange("c p t -> p c t")[
                    :, bass.ds(4 * j, 4), :]).then_inc(gates_landed, 16)

        def act_set_out(act, s):
            m_act.begin()
            for m in range(4):
                bank_ready(act, SETS_IN + s, m, R_OUT + 8 * s + 8)
                act.sem_inc(passed, 1)
                m_act.done(act.activation(mixed[:, bass.ds(4 * s + m, 1), :].rearrange("p a t -> p (a t)"),
                                          ps[:, m, 0:T], ACT.Copy), f"c{m}")
            act.wait_ge(m_act.sem, m_act.at(s, "c3"))
            act.wait_ge(m_vec.sem, m_vec.at(s - 1, "part"))
            act.sem_inc(passed, 1)
            m_act.done(act.activation(stage[1][:, :, :], mixed[:, bass.ds(4 * s, 4), :], ACT.Square), "sq")

        def vec_set_out(dve, s):
            m_vec.begin()
            dve.wait_ge(m_act.sem, m_act.at(s, "sq"))
            vec_squares(dve, stage[1], m_vec, s, "part", "sum")

        def vec_squares(dve, buf, st, rnd, part, total):
            st.done(dve.tensor_reduce(sq_part[:, :], buf[:, :, :].rearrange("p m t -> p t m"), AX_X, ALU.add), part)
            dve.wait_ge(st.sem, st.at(rnd, part))
            st.done(dve.tensor_tensor(sq_sum[:, :], sq_sum[:, :], sq_part[:, :], ALU.add), total)
            dve.wait_ge(st.sem, st.at(rnd, total))

        def act_out_set(act, s, first=False):
            for q in range(8):
                split_hi(act, R_OUT + 8 * s + q, q, R_OUT // 8 + s + 1)
                if q == 1:
                    act_merged(act, BLOCKS - 1) if first else act_set_out(act, s - 1)

        def vec_out_set(dve, s, first=False):
            for q in range(8):
                split_lo(dve, R_OUT + 8 * s + q, q)
                if first and q == 1:
                    vec_merge(dve, BLOCKS - 1)
                if first and q == 2:
                    vec_merged(dve, BLOCKS - 1)
                if not first and q == 3:
                    vec_set_out(dve, s - 1)

        def pe_out_set(pe, s, first=False):
            for q in range(8):
                if first and q in (0, 6):
                    pe.wait_ge(b_vec.sem, b_vec.last(BLOCKS - 2 if q == 0 else BLOCKS - 1))

                def free(m):
                    if not first:
                        pe.wait_ge(m_act.sem, m_act.at(s - 1, f"c{m}"))

                products(pe, R_OUT + 8 * s + q, q, lambda c: m_hi[:, 2 * q + c, :], lambda c: m_lo[:, 2 * q + c, :],
                         0, q, 8, free)

        HB = D_FF // 512

        def split_up(act, q):
            split_hi(act, R_UP + q, q, R_UP // 8 + 1)

        def act_hidden(act, j, first=False):
            for q in range(8 if first else 0, 16):
                split_hi(act, R_UP + 16 * j + q, q % 8, R_UP // 8 + 2 * j + q // 8 + 1)
                if first and q == 9:
                    e_act_root(act)
                if q == 10:
                    f_act.begin()
                    act.wait_ge(f_vec.sem, f_vec.at(j, "g"))
                    f_act.done(act.activation(stage[1][:, :, :], stage[0][:, :, :], ACT.Sigmoid), "e")

        def e_act_root(act):
            act.wait_ge(e_pe2.sem, e_pe2.at(0, "p3"))
            e_act.done(act.activation(rs_ffn[:, :], ps[:, 4, 0:T], ACT.Sqrt, scale=1.0 / D_MODEL,
                                      bias=eps_c[:, 0:1]), "rt2")

        def times_root(dve, dst, bank):
            return dve.tensor_tensor(dst[:, :, :], ps[:, bank:bank + 4, 0:T],
                                     rs_ffn[:, :].unsqueeze(1).broadcast_to([P, 4, T]), ALU.mult)

        def vec_hidden(dve, j, first=False):
            def chain(ins, name):
                f_vec.done(ins, name)
                dve.wait_ge(f_vec.sem, f_vec.at(j, name))

            for q in range(8 if first else 0, 16):
                split_lo(dve, R_UP + 16 * j + q, q % 8)
                if first and q == 9:
                    dve.wait_ge(e_act.sem, e_act.at(0, "rt2"))
                    e_vec.done(dve.reciprocal(rs_ffn[:, :], rs_ffn[:, :]), "rs2")
                    dve.wait_ge(e_vec.sem, e_vec.at(0, "rs2"))
                if not first and q == 1:
                    vec_up(dve, j - 1)
                if q == 9:
                    f_vec.begin()
                    dve.wait_ge(granule_used, R_UP + 16 * j + 8)
                    chain(times_root(dve, stage[0], 0), "g")
                if q == 11:
                    dve.wait_ge(f_act.sem, f_act.at(j, "e"))
                    chain(dve.tensor_tensor(stage[0][:, :, :], stage[0][:, :, :], stage[1][:, :, :], ALU.mult), "gs")

        def vec_up(dve, j):
            dve.wait_ge(granule_used, R_UP + 16 * j + 16)
            f_vec.done(times_root(dve, stage[1], 4), "u")
            dve.wait_ge(f_vec.sem, f_vec.at(j, "u"))
            f_vec.done(dve.tensor_tensor(hidden[:, bass.ds(4 * j, 4), :], stage[0][:, :, :], stage[1][:, :, :],
                                         ALU.mult), "act")
            dve.wait_ge(f_vec.sem, f_vec.at(j, "act"))

        def pe_hidden(pe, j, first=False):
            for q in range(16):
                if first and q < 8 and q % 2 == 0:
                    pe.wait_ge(e_vec.sem, e_vec.at(0, f"l{q // 2}"))
                if first and q == 8:
                    pe.wait_ge(e_act.sem, e_act.at(0, "rt2"))

                def free(m):
                    if m == 0 and not first:
                        pe.wait_ge(f_vec.sem, f_vec.at(j - 1, "g" if q < 8 else "u"))

                products(pe, R_UP + 16 * j + q, q % 8, lambda c: h2_hi[:, 2 * (q % 8) + c, :],
                         lambda c: h2_lo[:, 2 * (q % 8) + c, :], 4 * (q // 8), q % 8, 8, free, by_bank=False)
                if first and q < 8 and q % 2:
                    b = q // 2
                    pe.wait_ge(e_act.sem, e_act.at(0, f"sq{b}"))
                    for m in range(4):
                        ins = pe.matmul(ps[:, 4, 0:T], ones[:, :], stage[b % 2][:, m, :],
                                        start=q == 1 and m == 0, stop=q == 7 and m == 3)
                    e_pe2.done(ins, f"p{b}")

        DOWN = FT_N

        def down(eng, do):
            for pas in range(2):
                def one(k, q, i):
                    at = R_DOWN + DOWN * pas + q
                    do(pas, k, at + 8 * i, at % 8, at // 8 + i + 1, q)
                for k in range(4):
                    one(k, k, 0)
                with eng.Fori(0, (DOWN - 4) // 8) as i:
                    for q in range(4, 12):
                        one(8 * i + q, q, i)

        def act_out(act, pas):
            g_act.begin()
            for m in range(8):
                if m < 7:
                    act.wait_ge(down_done, 7 * (5 * pas + 4) + m + 1)
                else:
                    act.wait_ge(granule_used, R_DOWN + DOWN * (pas + 1))
                g_act.done(act.activation(ffn[:, 8 * pas + m, :], ps[:, m, 0:T], ACT.Copy), f"c{m}")

        def act_out_sq(act, pas):
            act.wait_ge(g_act.sem, g_act.at(pas, "c7"))
            if pas:
                act.wait_ge(g_vec.sem, g_vec.at(0, "s1"))
            for b in range(2):
                k = 8 * pas + 4 * b
                g_act.done(act.activation(stage[b][:, :, :], ffn[:, k:k + 4, :], ACT.Square), f"q{b}")

        def vec_out_sq(dve, pas):
            g_vec.begin()
            for b in range(2):
                dve.wait_ge(g_act.sem, g_act.at(pas, f"q{b}"))
                vec_squares(dve, stage[b], g_vec, pas, f"p{b}", f"s{b}")

        def r_use(r):
            return r // RAW + 1

        def sync_rest(sp):
            rounds(sp, sync_mix)
            with sp.Fori(0, BLOCKS) as j:
                for q in range(8):
                    load(sp, R_BRANCH + 8 * j + q, q, branch_w(j, q))
            with sp.Fori(0, BLOCKS) as j:
                for q in range(8):
                    load(sp, R_OUT + 8 * j + q, q, w_granule(w_out, q, j))
            with sp.Fori(0, HB) as j:
                for q in range(16):
                    load(sp, R_UP + 16 * j + q, q % 8, w_granule(w_up, q % 8, j if q < 8 else j + HB))
            down(sp, lambda pas, k, r, slot, use, q: load(sp, r, slot, w_dn.rearrange("(k p) n -> k p n", p=P)[
                bass.ds(k, 1), :, 1024 * pas:1024 * pas + 1024].rearrange("a p n -> (a p) n")))
            for t4 in range(4):
                for j, (t0, n) in enumerate(NT):
                    sp.wait_ge(y_act.sem, y_act.at(0, f"o{3 * t4 + j}"))
                    cols = slice(512 * t4, 512 * t4 + 512)
                    sp.dma_start(y_p[t0:t0 + n, cols] if j < 2 else y_s[:, cols], y_tok[0:n, j, cols]).then_inc(y_stored, 16)
            sp.wait_ge(y_stored, 16 * 12)
            sp.wait_ge(u_stored, 16 * SETS_IN)

        def act_rest(act):
            act.sem_inc(k_act.sem, len(k_act.names))
            act.sem_inc(v_act.sem, len(v_act.names))
            act.wait_ge(q_zero, 1)
            rounds(act, act_mix)
            act.wait_ge(v_vec.sem, v_vec.at(NB - 1, "o"))
            d_act.done(act.activation(s_flat.rearrange("p (h t) -> p h t", h=HEADS), o_da[:, :, SEQ:], ACT.Square), "sq")
            act_branch(act, 0, first=True)
            with act.Fori(1, BLOCKS) as j:
                act_branch(act, j)
            act_out_set(act, 0, first=True)
            with act.Fori(1, BLOCKS) as j:
                act_out_set(act, j)
            act_set_out(act, BLOCKS - 1)
            for q in range(2):
                split_up(act, q)
            act.wait_ge(e_pe.sem, e_pe.at(0, "ss"))
            e_act.done(act.activation(rs_mix[:, :], ps[:, 0, 0:T], ACT.Sqrt, scale=1.0 / D_MODEL,
                                      bias=eps_c[:, 0:1]), "rt")
            for b in range(4):
                act.wait_ge(e_vec.sem, e_vec.at(0, f"x{b}"))
                for g in range(4 * b, 4 * b + 4):
                    ins = act.activation(h2_hi[:, g, :], o_all[:, g, :], ACT.Copy, scale=nrm_w[:, 2, g:g + 1])
                e_act.done(ins, f"h{b}")
                if b >= 2:
                    act.wait_ge(e_pe2.sem, e_pe2.at(0, f"p{b - 2}"))
                e_act.done(act.activation(stage[b % 2][:, :, :], o_all[:, 4 * b:4 * b + 4, :], ACT.Square), f"sq{b}")
                if b < 3:
                    split_up(act, 2 * b + 2)
                    split_up(act, 2 * b + 3)
            act_hidden(act, 0, first=True)
            with act.Fori(1, HB) as j:
                act_hidden(act, j)
            act.wait_ge(f_vec.sem, f_vec.at(HB - 2, "act"))

            def granule(pas, k, r, slot, use, q):
                act.wait_ge(raw_landed[slot], 16 * use)
                act.wait_ge(granule_used, r - HALVES + 1)
                if q == 4:
                    act.wait_ge(f_vec.sem, f_vec.at(HB - 1, "act"))
                act.activation(hid_hi[slot % HALVES][:, :], hidden[:, bass.ds(k, 1), :].rearrange("p a t -> p (a t)"), ACT.Copy)
                act.activation(w_hi[slot % HALVES][:, :], raw[slot][:, :], ACT.Copy).then_inc(hi_ready, 1)
                if pas and q == 1:
                    act_out(act, 0)
                if pas and q == 3:
                    act_out_sq(act, 0)

            down(act, granule)
            act_out(act, 1)
            act_out_sq(act, 1)
            act.wait_ge(y_pe.sem, y_pe.at(0, "ss"))
            y_act.done(act.activation(rs_mix[:, :], ps[:, 0, 0:T], ACT.Sqrt, scale=1.0 / D_MODEL,
                                      bias=eps_c[:, 0:1]), "rt")
            for k in range(12):
                t4, j = k // 3, k % 3
                n = NT[j][1]
                act.wait_ge(y_pe.sem, y_pe.at(0, f"t{k}"))
                y_act.done(act.activation(y_tok[0:n, j, 512 * t4:512 * t4 + 512], ps[0:n, k % 8, :], ACT.Copy), f"o{k}")

        def vec_rest(dve):
            dve.sem_inc(k_vec.sem, len(k_vec.names))
            dve.sem_inc(v_vec.sem, len(v_vec.names))
            dve.wait_ge(h_pe.sem, h_pe.last(HEADS - 1))
            dve.wait_ge(h_act.sem, h_act.last(HEADS - 1))
            dve.wait_ge(h_pool.sem, h_pool.last(HEADS - 1))
            dve.wait_ge(granule_used, R_MIX)
            dve.memset(q_hi[:, :, :].bitcast(F32), 0.0)
            dve.memset(q_lo[:, :, :].bitcast(F32), 0.0).then_inc(q_zero, 1)
            dve.wait_ge(q_zero, 1)
            rounds(dve, vec_mix)
            vec_branch(dve, 0, first=True)
            with dve.Fori(1, BLOCKS) as j:
                vec_branch(dve, j)
            dve.sem_inc(m_vec.sem, len(m_vec.names))
            dve.memset(sq_sum[:, :], 0.0).then_inc(sums_zero, 1)
            dve.wait_ge(sums_zero, 1)
            vec_out_set(dve, 0, first=True)
            with dve.Fori(1, BLOCKS) as j:
                vec_out_set(dve, j)
            vec_set_out(dve, BLOCKS - 1)
            for q in range(2):
                split_lo(dve, R_UP + q, q)

            def chain(ins, name, st=e_vec):
                st.done(ins, name)
                dve.wait_ge(st.sem, st.at(0, name))

            dve.wait_ge(e_act.sem, e_act.at(0, "rt"))
            chain(dve.reciprocal(rs_mix[:, :], rs_mix[:, :]), "rs")
            dve.wait_ge(x_back, 16)
            for b in range(4):
                for g in range(4 * b, 4 * b + 4):
                    ins = dve.scalar_tensor_tensor(mixed[:, g, :], mixed[:, g, :], nrm_w[:, 1, g:g + 1],
                                                   rs_mix[:, :], ALU.mult, ALU.mult)
                four = slice(4 * b, 4 * b + 4)
                chain(ins, f"n{b}")
                chain(dve.tensor_tensor(o_all[:, four, :], o_all[:, four, :], mixed[:, four, :], ALU.add), f"x{b}")
                dve.wait_ge(e_act.sem, e_act.at(0, f"h{b}"))
                for g in range(4 * b, 4 * b + 4):
                    ins = dve.scalar_tensor_tensor(h2_lo[:, g, :], o_all[:, g, :], nrm_w[:, 2, g:g + 1],
                                                   h2_hi[:, g, :].bitcast(F32), ALU.mult, ALU.subtract)
                e_vec.done(ins, f"l{b}")
                if b < 3:
                    for q in (2 * b + 2, 2 * b + 3):
                        split_lo(dve, R_UP + q, q)
            vec_hidden(dve, 0, first=True)
            with dve.Fori(1, HB) as j:
                vec_hidden(dve, j)

            def granule(pas, k, r, slot, use, q):
                dve.wait_ge(hi_ready, r + 1)
                dve.tensor_tensor(hid_lo[slot % HALVES][:, :], hidden[:, bass.ds(k, 1), :].rearrange("p a t -> p (a t)"),
                                  hid_hi[slot % HALVES][:, :].bitcast(F32), ALU.subtract)
                dve.tensor_tensor(w_lo[slot % HALVES][:, :], raw[slot][:, :],
                                  w_hi[slot % HALVES][:, :].bitcast(F32), ALU.subtract).then_inc(lo_ready, 1)
                if not pas and q == 1:
                    vec_up(dve, HB - 1)
                    dve.memset(sq_sum[:, :], 0.0).then_inc(sums_zero, 1)
                    dve.wait_ge(sums_zero, 2)
                if pas and q == 3:
                    vec_out_sq(dve, 0)

            down(dve, granule)
            vec_out_sq(dve, 1)
            dve.wait_ge(y_act.sem, y_act.at(0, "rt"))
            chain(dve.reciprocal(rs_mix[:, :], rs_mix[:, :]), "rs", y_vec)
            for b in range(4):
                for g in range(4 * b, 4 * b + 4):
                    ins = dve.scalar_tensor_tensor(ffn[:, g, :], ffn[:, g, :], nrm_w[:, 3, g:g + 1],
                                                   rs_mix[:, :], ALU.mult, ALU.mult)
                four = slice(4 * b, 4 * b + 4)
                chain(ins, f"n{b}", y_vec)
                chain(dve.tensor_tensor(ffn[:, four, :], o_all[:, four, :], ffn[:, four, :], ALU.add), f"y{b}", y_vec)

        def pe_rest(pe):
            pe.sem_inc(k_pe.sem, len(k_pe.names))
            pe.sem_inc(v_pe.sem, len(v_pe.names))
            pe.sem_inc(v_used, HALVES)
            pe.wait_ge(set_out, 4 * SETS_IN)
            rounds(pe, pe_mix)
            pe.wait_ge(v_used, PAGES * NB + HALVES)
            pe.sem_inc(granule_used, R_BRANCH - R_MIX)
            pe_branch(pe, 0, first=True)
            with pe.Fori(1, BLOCKS) as j:
                pe_branch(pe, j)
            pe_out_set(pe, 0, first=True)
            with pe.Fori(1, BLOCKS) as j:
                pe_out_set(pe, j)
            pe.wait_ge(m_vec.sem, m_vec.last(BLOCKS - 1))
            e_pe.done(pe.matmul(ps[:, 0, 0:T], ones[:, :], sq_sum[:, :], start=True, stop=True), "ss")
            pe.wait_ge(e_act.sem, e_act.at(0, "rt"))
            pe_hidden(pe, 0, first=True)
            with pe.Fori(1, HB) as j:
                pe_hidden(pe, j)

            def down_granule(pas, k, r, slot, use, q):
                pe.wait_ge(lo_ready, r + 1)
                wh, wl = w_hi[slot % HALVES], w_lo[slot % HALVES]
                xh, xl = hid_hi[slot % HALVES][:, :], hid_lo[slot % HALVES][:, :]
                for m in range(8):
                    if pas and q == 0:
                        pe.wait_ge(g_act.sem, g_act.at(0, f"c{m}"))
                    if not pas and q == 0 and m in (0, 4):
                        pe.wait_ge(f_vec.sem, f_vec.at(HB - 1, "u" if m else "g"))
                    c = slice(P * m, P * m + P)
                    add = dict(start=False, stop=q > 3, skip_group_check=q > 3)
                    pe.matmul(ps[:, m, 0:T], wh[:, c], xh, **dict(add, start=q == 0))
                    pe.matmul(ps[:, m, 0:T], wl[:, c], xh, **add)
                    ins = pe.matmul(ps[:, m, 0:T], wh[:, c], xl, **dict(add, stop=q >= 3))
                    if q == 11 and m < 7:
                        ins.then_inc(down_done, 1)
                ins.then_inc(granule_used, 1)

            down(pe, down_granule)
            pe.wait_ge(g_vec.sem, g_vec.at(1, "s1"))
            y_pe.done(pe.matmul(ps[:, 0, 0:T], ones[:, :], sq_sum[:, :], start=True, stop=True), "ss")
            pe.wait_ge(y_act.sem, y_act.at(0, "rt"))
            for k in range(12):
                t4, j = k // 3, k % 3
                t0, n = NT[j]
                if j == 0:
                    pe.wait_ge(y_vec.sem, y_vec.at(0, f"y{t4}"))
                if k >= 8:
                    pe.wait_ge(y_act.sem, y_act.at(0, f"o{k - 8}"))
                for c in range(4):
                    ins = pe.transpose(ps[0:n, k % 8, P * c:P * c + P], ffn[:, 4 * t4 + c, t0:t0 + n], ident[:, :])
                y_pe.done(ins, f"t{k}")

        def pool_rest(pool):
            pool.wait_ge(h_pe.sem, h_pe.last(HEADS - 1))
            pool.wait_ge(h_vec.sem, h_vec.last(HEADS - 1))
            pool.wait_ge(granule_used, R_MIX)
            pool.dma_start(q_all[:, :, :], uT[DQT:DQT + 8].rearrange("c p t -> p c t")[:, :, SEQ:T]).then_inc(mix_landed, 16)
            rows = [[P * BIAS_L, MAPS]]
            pool.dma_start(near[:, :], bass.AP(bias_rows.tensor, P - 1, rows + [[BIAS_L - 1, NQ], [1, NEAR]])).then_inc(mix_landed, 16)
            pool.dma_start(far[:, :], bass.AP(bias_rows.tensor, 0, rows + [[BIAS_L, NQ], [1, 2]])).then_inc(mix_landed, 16)
            rounds(pool, pool_mix)
            pool.wait_ge(v_used, PAGES * NB + HALVES)
            pool.wait_ge(v_pe.sem, v_pe.last(NB - 1))
            pool.wait_ge(v_vec.sem, v_vec.last(NB - 1))
            pool_branch(pool, 0, first=True)
            with pool.Fori(1, BLOCKS) as j:
                pool_branch(pool, j)
            pool.wait_ge(d_vec.sem, d_vec.at(0, "dl"))
            pool.dma_start(o_all[:, :, :], xT_keep.rearrange("c p t -> p c t")).then_inc(x_back, 16)


        @block.sync
        def _(sp):
            for j, (t0, n) in enumerate(NT):
                sp.dma_start(x_tok[j][0:n, :], xp[t0:t0 + n, :] if j < 2 else xs).then_inc(x_landed[j], 16)
            for dst, src in ((ident[:], c_ident), (nrm_w[:], nrm), (hg_w[:], hgw), (coef[:], c_coef),
                             (lb_t[:, 0:2, :], lbl), (lam_in[:], lamv.broadcast_to([P, 4, DH])),
                             (hot[:], c_hot), (tab[0:32, :], table), (scan_keep[:], c_scan),
                             (causal[:], c_causal), (own[:], c_own), (pages[:], pt)):
                sp.dma_start(dst, src).then_inc(const_landed, 16)
            for r in range(RAW):
                load(sp, r, r, w_granule(w_in, r, 0), first=True)
            with sp.Fori(1, SETS_HEAD) as n:
                for q in range(8):
                    load(sp, 8 * n + q, q, w_granule(w_in, q, n))
            with sp.Fori(0, HEADS // 2) as i:
                for par in range(2):
                    h = 2 * i + par
                    n = SETS_HEAD + h
                    for q in range(8):
                        load(sp, 8 * n + q, q, w_granule(w_in, q, n))
                        if q == 4:
                            head_loads(sp, h, par)
            sync_rest(sp)

        @block.scalar
        def _(act):
            act.sem_inc(h_act.sem, 2 * len(h_act.names))
            act.wait_ge(u_pool.sem, u_pool.at(0, "zero"))
            for j, (t0, n) in enumerate(NT):
                act.wait_ge(x_landed[j], 16)
                if j:
                    act.wait_ge(u_act.sem, u_act.at(0, f"sq{j - 1}"))
                u_act.done(act.activation(x_sq[0:n, :], x_tok[j][0:n, :], ACT.Square,
                                          accum_out=x_rs[0:n, 0, j:j + 1]), f"sq{j}")
            act.wait_ge(u_pool.sem, u_pool.at(0, "mean"))
            u_act.done(act.activation(x_rs[:, 2, :], x_rs[:, 1, :], ACT.Sqrt), "root")
            act.wait_ge(u_vec.sem, u_vec.at(0, "lb_d"))
            u_act.done(act.activation(lb_t[:, 3:5, :], lb_t[:, 3:5, :], ACT.Exp), "lb_e")
            act.wait_ge(u_vec.sem, u_vec.at(0, "lam_d"))
            u_act.done(act.activation(lam_s[:, 2:4], lam_s[:, 0:2], ACT.Exp), "lam_e")
            for r in range(2):
                split_hi(act, r, r, 1, first=True)
            for g in tiles:
                act.wait_ge(u_pe.sem, u_pe.at(0, f"x{g}"))
                if g >= 8 and g % 4 == 0:
                    act.wait_ge(x_kept[g // 4 % 2], 16)
                u_act.done(act.activation(xT4[g // 4 % 2][:, g % 4, :], ps[:, 4 + g % 4, 0:T], ACT.Copy), f"x{g}")
                act.wait_ge(u_vec.sem, u_vec.at(0, f"h{g}"))
                u_act.done(act.activation(x_hi[:, g, :], hT[g % 2][:, :], ACT.Copy), f"h{g}")
                if g % 4 == 3:
                    act.wait_ge(u_act.sem, u_act.at(0, f"x{g}"))
                    act.dma_start(xT_keep[g - 3:g + 1].rearrange("c p t -> p c t"),
                                  xT4[g // 4 % 2][:, :, :]).then_inc(x_kept[g // 4 % 2], 16)
                if g > 1 and g % 2 and g < 15:
                    r = g // 2 + 1
                    split_hi(act, r, r, 1, first=r < HALVES)
            act_block(act, 1, 1)
            with act.Fori(1, SETS_HEAD // 2) as i:
                for par in range(2):
                    act_block(act, 2 * i + par, par)
            with act.Fori(0, HEADS // 2) as i:
                for par in range(2):
                    act_block(act, SETS_HEAD + 2 * i + par, par, (2 * i + par, i))
            read_set(act, SETS_IN - 1, R_MIX, 1)
            act_rest(act)

        @block.vector
        def _(dve):
            def chain(ins, name):
                u_vec.done(ins, name)
                dve.wait_ge(u_vec.sem, u_vec.at(0, name))

            dve.sem_inc(h_vec.sem, 2 * len(h_vec.names))
            dve.memset(eps_c[:, :], EPS)
            u_vec.done(dve.memset(ones[:, :], 1.0), "ones")
            dve.wait_ge(const_landed, CONSTS)
            u_vec.done(dve.memset(tab[32:33, :], -1e30), "tab")
            chain(dve.tensor_tensor(lb_t[:, 2, :], lb_t[:, 0, :], lb_t[:, 1, :], ALU.max), "lb_max")
            dve.tensor_tensor(lb_t[:, 3, :], lb_t[:, 0, :], lb_t[:, 2, :], ALU.subtract)
            u_vec.done(dve.tensor_tensor(lb_t[:, 4, :], lb_t[:, 1, :], lb_t[:, 2, :], ALU.subtract), "lb_d")
            lam4 = lam_in[:, :, :].rearrange("p (a b) d -> p b a d", b=2)
            chain(dve.tensor_tensor(lam_p[:, :, :], lam4[:, 0], lam4[:, 1], ALU.mult), "lam_p")
            u_vec.done(dve.tensor_reduce(lam_s[:, 0:2], lam_p[:, :, :], AX_X, ALU.add), "lam_d")
            dve.wait_ge(u_act.sem, u_act.at(0, "root"))
            chain(dve.reciprocal(x_rs[:, 2, :], x_rs[:, 2, :]), "rs_inv")
            for j in range(3):
                ins = dve.tensor_scalar(x_rsb[:, j, :], ones[:, :], x_rs[:, 2, j:j + 1], None, ALU.mult)
            u_vec.done(ins, "rsb")
            dve.wait_ge(u_pe.sem, u_pe.at(0, "bias"))
            u_vec.done(dve.tensor_copy(bias_vec[:, :], ps[0:MAPS, 6, 0:BIAS_L]), "bias_vec")
            dve.wait_ge(u_pe.sem, u_pe.at(0, "rs"))
            chain(dve.tensor_copy(rs_all[:, :], ps[:, 7, 0:T]), "rs")
            for g in tiles:
                dve.wait_ge(u_act.sem, u_act.at(0, f"x{g}"))
                if g >= 2:
                    dve.wait_ge(u_vec.sem, u_vec.at(0, f"l{g - 2}"))
                chain(dve.scalar_tensor_tensor(hT[g % 2][:, :], ps[:, 4 + g % 4, 0:T], nrm_w[:, 0, g:g + 1],
                                               rs_all[:, :], ALU.mult, ALU.mult), f"h{g}")
                dve.wait_ge(u_act.sem, u_act.at(0, f"h{g}"))
                u_vec.done(dve.tensor_tensor(x_lo[:, g, :], hT[g % 2][:, :],
                                             x_hi[:, g, :].bitcast(F32), ALU.subtract), f"l{g}")
                if g == 1:
                    split_lo(dve, 0, 0)
                if g % 2 and g < 15:
                    split_lo(dve, g // 2 + 1, g // 2 + 1)
            chain(dve.tensor_tensor(lb_t[:, 5, :], lb_t[:, 3, :], lb_t[:, 4, :], ALU.add), "lb_s")
            chain(dve.reciprocal(lb_t[:, 5, :], lb_t[:, 5, :]), "lb_r")
            chain(dve.tensor_tensor(lb, lb_t[:, 3, :], lb_t[:, 5, :], ALU.mult), "lb")
            u_vec.done(dve.tensor_scalar(omlb, lb, -1.0, 1.0, ALU.mult, ALU.add), "omlb")
            u_vec.done(dve.memset(aT[:, :, :], 0.0), "aT")
            chain(dve.tensor_tensor(lam_s[:, 4:5], lam_s[:, 2:3], lam_s[:, 3:4], ALU.subtract), "lam1")
            chain(dve.tensor_scalar(lam_s[:, 5:6], lam_s[:, 4:5], LAM_INIT, None, ALU.add), "lam2")
            u_vec.done(dve.tensor_scalar(neg_lam[:, :], lam_s[:, 5:6], -1.0, None, ALU.mult), "neg")
            chain(dve.scalar_tensor_tensor(cf[:, :], lam_s[:, 5:6], coef[:, 1:2], coef[:, 0:1],
                                           ALU.mult, ALU.add), "cf")
            with dve.Fori(1, SETS_HEAD) as n:
                for q in range(8):
                    split_lo(dve, 8 * n + q, q)
            with dve.Fori(0, HEADS // 2) as i:
                for par in range(2):
                    h = 2 * i + par
                    for q in range(8):
                        split_lo(dve, R_HEAD + 8 * h + q, q)
                        vec_head(dve, q, par, h, i)
            vec_rest(dve)

        @block.tensor
        def _(pe):
            pe.sem_inc(h_pe.sem, 2 * len(h_pe.names))
            pe.wait_ge(const_landed, CONSTS)
            pe.wait_ge(u_vec.sem, u_vec.at(0, "tab"))
            u_pe.done(pe.matmul(ps[0:MAPS, 6, 0:BIAS_L], tab[:, :], hot[:, :], start=True, stop=True), "bias")

            def turn(g):
                if g >= 4:
                    pe.wait_ge(u_act.sem, u_act.at(0, f"x{g - 4}"))
                    pe.wait_ge(u_vec.sem, u_vec.at(0, f"h{g - 4}"))
                for j, (t0, n) in enumerate(NT):
                    ins = pe.transpose(ps[:, 4 + g % 4, t0:t0 + n], x_tok[j][0:n, g * P:(g + 1) * P],
                                       ident[0:n, 0:n])
                u_pe.done(ins, f"x{g}")

            for j in range(3):
                pe.wait_ge(x_landed[j], 16)
            pe.wait_ge(u_vec.sem, u_vec.at(0, "rsb"))
            for j, (t0, n) in enumerate(NT):
                ins = pe.matmul(ps[:, 7, t0:t0 + n], x_rsb[0:n, j, :], ident[0:n, 0:n], start=True, stop=True)
            u_pe.done(ins, "rs")
            def in_products(r, q, free):
                products(pe, r, q, lambda c: x_hi[:, 2 * q + c, :], lambda c: x_lo[:, 2 * q + c, :],
                         0, q, 8, free)

            for g in range(4):
                if g == 2:
                    pe.wait_ge(u_vec.sem, u_vec.at(0, "rs"))
                turn(g)
            for q in range(8):
                pe.wait_ge(u_vec.sem, u_vec.at(0, f"l{2 * q + 1}"))
                in_products(q, q, lambda m: None)
                for g in (2 * q + 4, 2 * q + 5):
                    if g < KT:
                        turn(g)
            with pe.Fori(1, SETS_HEAD) as n:
                for q in range(8):
                    in_products(8 * n + q, q, lambda m: pe.wait_ge(set_out, 4 * n + m - 3))
            with pe.Fori(0, HEADS // 2) as i:
                for par in range(2):
                    h = 2 * i + par
                    n = SETS_HEAD + h
                    for q in range(8):
                        in_products(8 * n + q, q, lambda m: pe.wait_ge(set_out, 4 * n + m - 3))
                        pe_head(pe, q, par, h, i)
            pe_rest(pe)

        @block.gpsimd
        def _(pool):
            pool.sem_inc(h_pool.sem, 2)
            pool.sem_inc(stage_free, 2)
            u_pool.done(pool.memset(x_rs[:, :, :], 1.0), "zero")
            pool.wait_ge(u_act.sem, u_act.at(0, "sq2"))
            u_pool.done(pool.tensor_scalar(x_rs[:, 1, :], x_rs[:, 0, :], 1.0 / D_MODEL, EPS, ALU.mult, ALU.add), "mean")
            pool.wait_ge(u_vec.sem, u_vec.at(0, "bias_vec"))
            pool.dma_start(bias_rows, bias_vec[:, :].unsqueeze(1).broadcast_to([MAPS, P, BIAS_L])).then_inc(bias_stored, 16)
            store_set(pool, 0, 0)
            with pool.Fori(0, (SETS_HEAD - 2) // 2) as i:
                for par in range(2):
                    store_set(pool, 2 * i + 1 + par, 1 - par)
            with pool.Fori(0, HEADS // 2) as i:
                for par in range(2):
                    h = 2 * i + par
                    store_set(pool, SETS_HEAD - 1 + h, 1 - par)
                    pool_head(pool, par, h)
            store_set(pool, SETS_IN - 1, 1)
            pool_rest(pool)


def bucket(dist):
    import math

    import numpy as np
    near = 16
    n = np.float32(max(dist, 1))
    far = near + int(np.log(n / np.float32(near)) / np.float32(math.log(128 / near)) * np.float32(near))
    return dist if dist < near else min(far, 31)


def kernel(**inputs):
    import numpy as np

    import concourse.bacc as bacc
    from concourse.bass_utils import run_bass_kernel_spmd

    a = {k: np.asarray(v) for k, v in inputs.items()}

    def cols(v):
        return v.reshape(-1, P).T

    scan = np.ones((P, T), np.float32)
    scan[:, 0:SEQ:CHUNK] = 0
    scan[:, SEQ::NQ] = 0
    i = np.arange(CHUNK)
    tri = (i[:, None] <= i[None, :]).astype(np.int32)
    same = (i[:, None] // NQ == i[None, :] // NQ).astype(np.int32)
    hot = np.zeros((33, BIAS_L), np.float32)
    for j in range(BIAS_L):
        dist = 255 - j
        hot[32 if dist < 0 else bucket(dist), j] = 1
    coef = np.zeros((P, 2), np.float32)
    coef[:CHUNK, 0], coef[CHUNK:, 1] = 1, -1
    arrays = {
        "xp": a["x_prompt"][0], "xs": a["x_sample"].reshape(NB * NQ, D_MODEL),
        "ck": a["cache_k"][0].reshape(POOL, PAGE, MAPS * DH), "cv": a["cache_v"][0].reshape(POOL, PAGE, HEADS * DV),
        "st": a["state_hgrn"][0], "pt": a["page_table"].astype(np.int32),
        "w_in": a["w_in"][0], "w_hg": a["w_branch_hg"][0], "w_da": a["w_branch_da"][0], "w_out": a["w_out"][0],
        "w_up": a["w_ffn_up"][0], "w_dn": a["w_ffn_down"][0],
        "nrm": np.stack([cols(a[k][0]) for k in ("norm_mix_pre", "norm_mix_post", "norm_ffn_pre", "norm_ffn_post")], 1),
        "hgw": np.stack([a["hg_norm_w"][0], a["da_subln_w"][0]], 1),
        "lbl": np.stack([cols(v) for v in a["hg_lb_logits"]], 1),
        "lamv": np.stack([a[f"da_lambda_{k}"][0] for k in ("q1", "k1", "q2", "k2")])[None],
        "table": a["rel_bias_table"],
        "c_ident": np.eye(P, dtype=np.float32), "c_scan": scan,
        "c_causal": np.stack([tri] * 4 + [tri * same], 1),
        "c_own": (i[:, None] // NQ == np.arange(NB)[None, :]).astype(np.float32),
        "c_hot": hot, "c_coef": coef,
    }
    outs = {"y_p": (SEQ, D_MODEL), "y_s": (NB * NQ, D_MODEL), "k_p": (SEQ, MAPS, DH), "v_p": (SEQ, HEADS, DV),
            "h_p": (HEADS, P, DV), "k_s": (NB * NQ, MAPS, DH), "v_s": (NB * NQ, HEADS, DV),
            "h_s": (NB, HEADS, P, DV)}
    nc = bacc.Bacc("TRN2", target_bir_lowering=False, num_devices=1)
    arrays = {k: np.ascontiguousarray(v) for k, v in arrays.items()}
    args = [nc.dram_tensor(k, v.shape, mybir.dt.from_np(v.dtype), kind="ExternalInput").ap() for k, v in arrays.items()]
    args += [nc.dram_tensor(k, s, F32, kind="ExternalOutput").ap() for k, s in outs.items()]
    build(nc, *args)
    r = run_bass_kernel_spmd(nc, [arrays], core_ids=[0]).results[0]
    return (r["y_p"].reshape(1, SEQ, D_MODEL), r["y_s"].reshape(NB, NQ, D_MODEL),
            r["k_p"].reshape(1, 1, SEQ, MAPS, DH), r["v_p"].reshape(1, 1, SEQ, HEADS, DV),
            r["h_p"].reshape(1, 1, HEADS, P, DV), r["k_s"].reshape(1, NB, NQ, MAPS, DH),
            r["v_s"].reshape(1, NB, NQ, HEADS, DV), r["h_s"].reshape(1, NB, HEADS, P, DV))
```
